# Optimizing a Trainium2 kernel written in Bass

```python
import jax
import jax.numpy as jnp
from jax import lax
import numpy as np

D_MODEL = 1024
BATCH = 1
SEQ = 512
DEPTH = 4
DEC_BATCH = 8
DEC_SEQ = 4
PAST_LEN = 1024
PAGE_SIZE = 128

N_MIXERS = 3
N_GLA_LAYERS = (DEPTH + 2) // 3
N_DSA_LAYERS = (DEPTH + 1) // 3
N_POOL_LAYERS = DEPTH // 3
RMS_EPS = 1e-6

GLA_HEADS = 4
GLA_KEY_DIM = D_MODEL // 2
GLA_VAL_DIM = D_MODEL
GLA_DK = GLA_KEY_DIM // GLA_HEADS
GLA_DV = GLA_VAL_DIM // GLA_HEADS
GLA_GATE_RANK = 16
GLA_GATE_TAU = 16.0
GLA_CHUNK = 64
GLA_IN = 2 * GLA_KEY_DIM + 2 * GLA_VAL_DIM + GLA_GATE_RANK

DSA_HEAD_DIM = 128
DSA_HEADS = D_MODEL // DSA_HEAD_DIM
DSA_WIDTH = DSA_HEADS * DSA_HEAD_DIM
IDX_HEADS = 4
IDX_DIM = 64
DSA_TOPK = 256
DSA_QBLOCK = 64
DSA_IN = 4 * DSA_WIDTH + IDX_HEADS * IDX_DIM + IDX_DIM + IDX_HEADS

POOL_WINDOWS = (2, 4, 8, 16)
POOL_GROUPS = len(POOL_WINDOWS)
POOL_WIDTH = D_MODEL
POOL_GROUP_WIDTH = POOL_WIDTH // POOL_GROUPS
POOL_STATE = max(POOL_WINDOWS) - 1

kernel_name = 'hybrid_gla_dsa_pool_decode_step'

def _split(x, sizes):
    offsets = [int(o) for o in np.cumsum(sizes)[:-1]]
    return jnp.split(x, offsets, axis=-1)

def take_rows(a, idx):
    return jax.vmap(lambda ab, ib: ab[ib])(a, idx)

def rmsnorm(x, g):
    xf = x.astype(jnp.float32)
    y = xf * lax.rsqrt(jnp.mean(xf * xf, axis=-1, keepdims=True) + RMS_EPS)
    return (y * g.astype(jnp.float32)).astype(x.dtype)

def gla_recurrence(q, k, v, logf, s0):
    B, L, H, _ = q.shape
    c = min(GLA_CHUNK, L)
    pad = (-L) % c
    n = (L + pad) // c

    def prep(t):
        t = jnp.pad(t.astype(jnp.float32), ((0, 0), (0, pad), (0, 0), (0, 0)))
        return t.reshape(B, n, c, H, t.shape[-1]).transpose(1, 0, 3, 2, 4)

    tri = jnp.tril(jnp.ones((c, c), dtype=bool))

    def step(s, inp):
        qc, kc, vc, gc = inp
        b = jnp.cumsum(gc, axis=2)
        diff = b[:, :, :, None, :] - b[:, :, None, :, :]
        decay = jnp.exp(jnp.where(tri[:, :, None], diff, -jnp.inf))
        att = jnp.einsum('bhtd,bhsd,bhtsd->bhts', qc, kc, decay)
        b_end = b[:, :, -1, :]
        o = (jnp.einsum('bhts,bhsv->bhtv', att, vc)
             + jnp.einsum('bhtd,bhdv->bhtv', qc * jnp.exp(b), s))
        s = (jnp.exp(b_end)[..., None] * s
             + jnp.einsum('bhsd,bhsv->bhdv', kc * jnp.exp(b_end[:, :, None, :] - b), vc))
        return s, o

    s, o = lax.scan(step, s0.astype(jnp.float32), (prep(q), prep(k), prep(v), prep(logf)))
    o = o.transpose(1, 0, 3, 2, 4).reshape(B, n * c, H, v.shape[-1])[:, :L]
    return o, s

def gla_mixer(h, s0, w_in, w_a2, b_a, g_on, w_out):
    B, L, _ = h.shape
    q, k, v, g, a = _split(h @ w_in, [GLA_KEY_DIM, GLA_KEY_DIM, GLA_VAL_DIM, GLA_VAL_DIM, GLA_GATE_RANK])
    logf = jax.nn.log_sigmoid((a @ w_a2 + b_a).astype(jnp.float32)) / GLA_GATE_TAU
    heads = lambda t, d: t.reshape(B, L, GLA_HEADS, d)
    o, s = gla_recurrence(heads(q, GLA_DK) * (GLA_DK ** -0.5), heads(k, GLA_DK),
                          heads(v, GLA_DV), heads(logf, GLA_DK), s0)
    o = rmsnorm(o, g_on).astype(h.dtype).reshape(B, L, GLA_VAL_DIM)
    return (o * jax.nn.silu(g)) @ w_out, s

def indexer_select(iq, iw, ik, q_pos, k_pos, topk):
    s = jnp.einsum('bqhd,bsd->bqhs', iq, ik, preferred_element_type=jnp.float32) * (IDX_DIM ** -0.5)
    score = jnp.einsum('bqh,bqhs->bqs', iw.astype(jnp.float32) * (IDX_HEADS ** -0.5), jax.nn.relu(s))
    causal = k_pos[None, :] <= q_pos[:, None]
    score = jnp.where(causal[None], score, -jnp.inf)
    _, idx = lax.top_k(score, topk)
    valid = idx <= q_pos[None, :, None]
    return idx, valid

def sparse_attend(q, k_sel, v_sel, valid):
    s = jnp.einsum('bqhd,bqkhd->bqhk', q, k_sel, preferred_element_type=jnp.float32) * (DSA_HEAD_DIM ** -0.5)
    s = jnp.where(valid[:, :, None, :], s, -jnp.inf)
    p = jax.nn.softmax(s, axis=-1)
    return jnp.einsum('bqhk,bqkhd->bqhd', p.astype(v_sel.dtype), v_sel)

def dsa_project(h, w_in):
    B, L, _ = h.shape
    q, k, v, g, iq, ik, iw = _split(h @ w_in, [DSA_WIDTH] * 4 + [IDX_HEADS * IDX_DIM, IDX_DIM, IDX_HEADS])
    hd = lambda t: t.reshape(B, L, DSA_HEADS, DSA_HEAD_DIM)
    return hd(q), hd(k), hd(v), g, iq.reshape(B, L, IDX_HEADS, IDX_DIM), ik, iw

def dsa_prompt_attend(q, k, v, iq, iw, ik):
    B, L = q.shape[:2]
    topk = min(DSA_TOPK, L // 4)
    qb = min(DSA_QBLOCK, L)
    nb = L // qb
    blocks = lambda t: jnp.swapaxes(t.reshape((B, nb, qb) + t.shape[2:]), 0, 1)
    pos = jnp.arange(L)

    def body(args):
        q_b, iq_b, iw_b, p_b = args
        idx, valid = indexer_select(iq_b, iw_b, ik, p_b, pos, topk)
        return sparse_attend(q_b, take_rows(k, idx), take_rows(v, idx), valid)

    out = lax.map(body, (blocks(q), blocks(iq), blocks(iw), pos.reshape(nb, qb)))
    return jnp.swapaxes(out, 0, 1).reshape(q.shape)

def dsa_sample_attend(q, k_new, v_new, iq, iw, ik_new, cache_k, cache_v, cache_ik, page_table):
    DB, DQ = q.shape[:2]
    ps = cache_k.shape[1]
    past = page_table.shape[1] * ps
    L = past + DQ
    topk = min(DSA_TOPK, L // 4)
    ik_past = cache_ik[page_table].reshape(DB, past, IDX_DIM).astype(ik_new.dtype)
    ik_all = jnp.concatenate([ik_past, ik_new], axis=1)
    q_pos = past + jnp.arange(DQ)
    idx, valid = indexer_select(iq, iw, ik_all, q_pos, jnp.arange(L), topk)
    is_new = (idx >= past)[..., None, None]
    p_pos = jnp.minimum(idx, past - 1)
    phys = take_rows(page_table, p_pos // ps)
    off = p_pos % ps
    n_pos = jnp.clip(idx - past, 0, DQ - 1)
    k_sel = jnp.where(is_new, take_rows(k_new, n_pos), cache_k[phys, off].astype(k_new.dtype))
    v_sel = jnp.where(is_new, take_rows(v_new, n_pos), cache_v[phys, off].astype(v_new.dtype))
    return sparse_attend(q, k_sel, v_sel, valid)

def dsa_out(o, g, w_out):
    B, L = o.shape[:2]
    return (o.reshape(B, L, DSA_WIDTH) * jax.nn.silu(g)) @ w_out

def pool_mixer(h, prefix, start_pos, w_in, w_grp, scale, w_out):
    B, L, _ = h.shape
    u, g = _split(h @ w_in, [POOL_WIDTH, POOL_WIDTH])
    ext = jnp.concatenate([prefix.astype(u.dtype), u], axis=1)
    P = POOL_STATE
    cs = jnp.cumsum(ext.astype(jnp.float32), axis=1)
    cs = jnp.pad(cs, ((0, 0), (1, 0), (0, 0)))
    pos = start_pos + jnp.arange(L)
    uf = u.astype(jnp.float32)
    diffs = []
    for gi, w in enumerate(POOL_WINDOWS):
        sl = slice(gi * POOL_GROUP_WIDTH, (gi + 1) * POOL_GROUP_WIDTH)
        win_sum = cs[:, P + 1:P + 1 + L, sl] - cs[:, P + 1 - w:P + 1 - w + L, sl]
        cnt = jnp.minimum(w, pos + 1).astype(jnp.float32)
        diffs.append(win_sum / cnt[None, :, None] - uf[..., sl])
    d = jnp.stack(diffs, axis=2).astype(u.dtype)
    y = jnp.einsum('blgc,gcd->blgd', d, w_grp).reshape(B, L, POOL_WIDTH) * scale
    return (y * jax.nn.silu(g)) @ w_out, ext[:, -P:]

def setup_inputs(seed: int = 0) -> dict:
    key = jax.random.key(seed)
    ks = jax.random.split(key, 24)
    f32 = jnp.float32
    n_pages = PAST_LEN // PAGE_SIZE
    n_used = DEC_BATCH * n_pages
    n_phys = n_used + max(1, n_used // 4)
    nrm = lambda k, shape, s=1.0: s * jax.random.normal(k, shape, f32)
    gain = lambda k, shape: 1.0 + 0.02 * jax.random.normal(k, shape, f32)
    page_table = jax.random.permutation(ks[7], n_phys)[:n_used].reshape(DEC_BATCH, n_pages).astype(jnp.int32)
    return {
        'x_prompt': nrm(ks[0], (BATCH, SEQ, D_MODEL)),
        'x_sample': nrm(ks[1], (DEC_BATCH, DEC_SEQ, D_MODEL)),
        'state_gla': nrm(ks[2], (N_GLA_LAYERS, DEC_BATCH, GLA_HEADS, GLA_DK, GLA_DV)),
        'cache_k': nrm(ks[3], (N_DSA_LAYERS, n_phys, PAGE_SIZE, DSA_HEADS, DSA_HEAD_DIM)),
        'cache_v': nrm(ks[4], (N_DSA_LAYERS, n_phys, PAGE_SIZE, DSA_HEADS, DSA_HEAD_DIM)),
        'cache_idx_k': nrm(ks[5], (N_DSA_LAYERS, n_phys, PAGE_SIZE, IDX_DIM)),
        'state_pool': nrm(ks[6], (N_POOL_LAYERS, DEC_BATCH, POOL_STATE, POOL_WIDTH)),
        'page_table': page_table,
        'gla_norm': gain(ks[8], (N_GLA_LAYERS, D_MODEL)),
        'gla_w_in': nrm(ks[9], (N_GLA_LAYERS, D_MODEL, GLA_IN), D_MODEL ** -0.5),
        'gla_w_a2': nrm(ks[10], (N_GLA_LAYERS, GLA_GATE_RANK, GLA_KEY_DIM), GLA_GATE_RANK ** -0.5),
        'gla_b_a': nrm(ks[11], (N_GLA_LAYERS, GLA_KEY_DIM), 0.1),
        'gla_out_norm': gain(ks[12], (N_GLA_LAYERS, GLA_DV)),
        'gla_w_out': nrm(ks[13], (N_GLA_LAYERS, GLA_VAL_DIM, D_MODEL), GLA_VAL_DIM ** -0.5),
        'dsa_norm': gain(ks[14], (N_DSA_LAYERS, D_MODEL)),
        'dsa_w_in': nrm(ks[15], (N_DSA_LAYERS, D_MODEL, DSA_IN), D_MODEL ** -0.5),
        'dsa_w_out': nrm(ks[16], (N_DSA_LAYERS, DSA_WIDTH, D_MODEL), DSA_WIDTH ** -0.5),
        'pool_norm': gain(ks[17], (N_POOL_LAYERS, D_MODEL)),
        'pool_w_in': nrm(ks[18], (N_POOL_LAYERS, D_MODEL, 2 * POOL_WIDTH), D_MODEL ** -0.5),
        'pool_w_grp': nrm(ks[19], (N_POOL_LAYERS, POOL_GROUPS, POOL_GROUP_WIDTH, POOL_GROUP_WIDTH), POOL_GROUP_WIDTH ** -0.5),
        'pool_scale': gain(ks[20], (N_POOL_LAYERS, POOL_WIDTH)),
        'pool_w_out': nrm(ks[21], (N_POOL_LAYERS, POOL_WIDTH, D_MODEL), POOL_WIDTH ** -0.5),
        'final_norm': gain(ks[22], (D_MODEL,)),
    }

def reference(x_prompt, x_sample, state_gla, cache_k, cache_v, cache_idx_k, state_pool, page_table,
              gla_norm, gla_w_in, gla_w_a2, gla_b_a, gla_out_norm, gla_w_out,
              dsa_norm, dsa_w_in, dsa_w_out,
              pool_norm, pool_w_in, pool_w_grp, pool_scale, pool_w_out, final_norm):
    B = x_prompt.shape[0]
    yp, ys = x_prompt, x_sample
    gla_sp, gla_ss, kp, ks_, vp, vs, ikp, iks, pool_sp, pool_ss = [], [], [], [], [], [], [], [], [], []
    for i in range(DEPTH):
        kind, j = i % N_MIXERS, i // N_MIXERS
        if kind == 0:
            w = (gla_w_in[j], gla_w_a2[j], gla_b_a[j], gla_out_norm[j], gla_w_out[j])
            s0 = jnp.zeros((B, GLA_HEADS, GLA_DK, GLA_DV), jnp.float32)
            dp, sp = gla_mixer(rmsnorm(yp, gla_norm[j]), s0, *w)
            ds, ss = gla_mixer(rmsnorm(ys, gla_norm[j]), state_gla[j], *w)
            gla_sp.append(sp)
            gla_ss.append(ss)
        elif kind == 1:
            q, k, v, g, iq, ik, iw = dsa_project(rmsnorm(yp, dsa_norm[j]), dsa_w_in[j])
            dp = dsa_out(dsa_prompt_attend(q, k, v, iq, iw, ik), g, dsa_w_out[j])
            kp.append(k)
            vp.append(v)
            ikp.append(ik)
            q, k, v, g, iq, ik, iw = dsa_project(rmsnorm(ys, dsa_norm[j]), dsa_w_in[j])
            o = dsa_sample_attend(q, k, v, iq, iw, ik, cache_k[j], cache_v[j], cache_idx_k[j], page_table)
            ds = dsa_out(o, g, dsa_w_out[j])
            ks_.append(k)
            vs.append(v)
            iks.append(ik)
        else:
            w = (pool_w_in[j], pool_w_grp[j], pool_scale[j], pool_w_out[j])
            hp = rmsnorm(yp, pool_norm[j])
            prefix0 = jnp.zeros((B, POOL_STATE, POOL_WIDTH), hp.dtype)
            dp, sp = pool_mixer(hp, prefix0, 0, *w)
            ds, ss = pool_mixer(rmsnorm(ys, pool_norm[j]), state_pool[j], PAST_LEN, *w)
            pool_sp.append(sp)
            pool_ss.append(ss)
        yp = yp + dp.astype(yp.dtype)
        ys = ys + ds.astype(ys.dtype)
    y_prompt = rmsnorm(yp, final_norm)
    y_sample = rmsnorm(ys, final_norm)
    gla_state_prompt = jnp.stack(gla_sp)
    gla_state_sample = jnp.stack(gla_ss)
    k_rows_prompt = jnp.stack(kp)
    k_rows_sample = jnp.stack(ks_)
    v_rows_prompt = jnp.stack(vp)
    v_rows_sample = jnp.stack(vs)
    idxk_rows_prompt = jnp.stack(ikp)
    idxk_rows_sample = jnp.stack(iks)
    pool_state_prompt = jnp.stack(pool_sp)
    pool_state_sample = jnp.stack(pool_ss)
    return (y_prompt, y_sample, gla_state_prompt, gla_state_sample, k_rows_prompt, k_rows_sample,
            v_rows_prompt, v_rows_sample, idxk_rows_prompt, idxk_rows_sample,
            pool_state_prompt, pool_state_sample)


_drawn_inputs = setup_inputs


def setup_inputs(seed=0):
    import zlib

    import numpy as np

    out = dict(_drawn_inputs(seed))
    spreads = {}
    factors = {'gla_out_norm': 3.062,
     'dsa_norm': 2.874,
     'pool_norm': 2.846,
     'pool_scale': 5.848,
     'final_norm': 2.789}
    for name, (base, spread) in spreads.items():
        noise = np.random.default_rng([zlib.crc32(name.encode()), seed]).standard_normal(out[name].shape)
        drawn = base * np.exp(spread * noise) if base else spread * noise
        out[name] = jnp.asarray(drawn.astype(out[name].dtype))
    for name, factor in factors.items():
        out[name] = (out[name] * factor).astype(out[name].dtype)
    return out
```

```python
from contextlib import ExitStack

import concourse.bass as bass
from concourse import mybir

F32 = mybir.dt.float32
F32R = mybir.dt.float32r
BF16 = mybir.dt.bfloat16
I32 = mybir.dt.int32
ALU = mybir.AluOpType
ACT = mybir.ActivationFunctionType
AX = mybir.AxisListType

P = 128
D = 1024
KT = D // P
SEQ, DB, DQ = 512, 8, 4
NS = DB * DQ
NP_T = SEQ // P
TILES = NP_T + 1
SMP = NP_T
TOK = SEQ + NS
HC = TOK // 2
PARTS = ((0, slice(0, HC)), (1, slice(HC, TOK)))
BLK = 512
HALF = 256
PAST, PAGE = 1024, 128
NPAGE = PAST // PAGE
RMS_EPS = 1e-6
GH, GDK, GDV = 4, 128, 256
CH = 64
NCH = SEQ // CH
TAU = 16.0
RANK = 16
DH, HD = 8, 128
IH, ID = 4, 64
TOPK_P, TOPK_S = 128, 256
KEYS = PAST + NS
WINDOWS = (2, 4, 8, 16)
STATE = 15
PADW = 16
FUTURE = -1e30
TAKEN = -3e38
NBANK = 8
RAW = 3
EXP_LN = "natural_log_exp_and_others"
KINDS = (0, 1, 2, 0)


def rows(t):
    return NS if t == SMP else P


def cols(t):
    return slice(t * P, t * P + rows(t))


class Plan:

    def __init__(self):
        self.value, self.bank = {}, {}


def program(nc, plan, x_prompt, x_sample, state_gla, cache_k, cache_v, cache_idx_k, state_pool, page_table,
            gla_norm, gla_w_in, gla_w_a2, gla_b_a, gla_out_norm, gla_w_out, dsa_norm, dsa_w_in, dsa_w_out,
            pool_norm, pool_w_in, pool_w_grp, pool_scale, pool_w_out, final_norm, outs):
    (y_prompt, y_sample, gla_state_prompt, gla_state_sample, k_rows_prompt, k_rows_sample, v_rows_prompt,
     v_rows_sample, idxk_rows_prompt, idxk_rows_sample, pool_state_prompt, pool_state_sample) = outs

    with ExitStack() as ctx:
        sems, count = {}, {}

        def semaphore(name):
            if name not in sems:
                sems[name] = ctx.enter_context(nc.semaphore(name))
            return sems[name]

        def sig(name, *key, also=(), n=1):
            s = semaphore(name)
            count[name] = count.get(name, 0) + n
            for k in (key, ("all",)) + tuple(also):
                plan.value[(name,) + k] = count[name]
            return s, n

        def on(name, *key):
            return semaphore(name), plan.value.get((name,) + key, 1)

        def bank_of(*key):
            return plan.bank.get(key, 0)

        place = {"at": (nc.sbuf_base + 63) // 64 * 64}

        def at(name, shape, dt, offset):
            return nc.alloc_sbuf_tensor_at(name, shape, dt, offset=offset)

        def size(shape, dt):
            n = 2 if dt == BF16 else 4
            for s in shape[1:]:
                n *= s
            return (n + 63) // 64 * 64

        def sb(name, shape, dt=F32):
            o = place["at"]
            place["at"] += size(shape, dt)
            return at(name, shape, dt, o)

        class Region:

            def __init__(self, start, end):
                self.o, self.end = start, end

            def __call__(self, name, shape, dt=F32):
                o = self.o
                self.o += size(shape, dt)
                assert self.o <= self.end, (name, self.o - self.end)
                return at(name, shape, dt, o)

        X = sb("X", [P, TILES, D])
        h_hi = sb("h_hi", [P, KT, TOK], F32R)
        h_lo = sb("h_lo", [P, KT, TOK], F32R)
        raw = sb("raw", [P, RAW, 2048])
        w_hi = sb("w_hi", [P, 2, 2048], F32R)
        w_lo = sb("w_lo", [P, 2, 2048], F32R)
        ident = sb("ident", [P, P])
        chunk_tri = sb("chunk_tri", [P, P])
        seq_tri = sb("seq_tri", [NS, NS])
        future_p = sb("future_p", [P, P])
        future_s = sb("future_s", [NS, NS])
        stack4 = sb("stack4", [P, NS])
        pick_tok = sb("pick_tok", [NS, DB, NS], BF16)
        seq_col = sb("seq_col", [P, DB, NS], BF16)
        seq_row = sb("seq_row", [NS, DB])
        no_reset = sb("no_reset", [P, TOK], BF16)
        inv_cnt = sb("inv_cnt", [P, PADW])
        cnt_i = sb("cnt_i", [P, PADW])
        b_a = sb("b_a", [P, GH])
        g_on = sb("g_on", [P, GDV])
        w_a2 = sb("w_a2", [RANK, GH * GDK])
        scale_p = sb("scale_p", [P, KT])
        eps = sb("eps", [P, 1])
        one = sb("one", [P, 1])
        ptab = sb("ptab", [1, DB * NPAGE], I32)
        st = sb("st", [P, 2, 8])
        ost = sb("ost", [P, 5, 20])
        sq_junk = sb("sq_junk", [P, D], BF16)
        gain_at = place["at"]
        gain = sb("gain", [P, D])
        xn_at = place["at"]
        xn = sb("xn", [P, 2, D])
        place["at"] += 128
        xn_end = place["at"]
        arena, arena_end = place["at"], nc.sbuf_usable_end

        g = Region(arena, arena_end)
        qg = g("gla_q", [P, GH, TOK])
        kg = g("gla_k", [P, GH, TOK])
        ktok_at = g.o
        k_tok = g("gla_k_tok", [P, TILES, GH * GDK])
        soft = at("gla_soft", [P, GH, TOK], F32, ktok_at)
        gate_g = g("gla_gate", [P, KT, TOK])
        v_g = g("gla_v", [P, TILES, D])
        s_now = g("gla_s_now", [P, 2, GH * GDV])
        s_in = g("gla_s_in", [P, 3, GH, GDV])
        att_g = g("gla_att", [P, GH, P])
        a_t = at("gla_a", [RANK, TOK], F32, g.o)
        q_seq = g("gla_q_seq", [P, GH, DB, NS])
        mid = g("gla_mid", [P, GH, NCH])
        fac = g("gla_fac", [P, GH, 2 * NCH])
        gx = Region(xn_at, xn_end)
        s_sum = gx("gla_s_sum", [P, GH * GDV])
        k_seq = gx("gla_k_seq", [NS, 2, GH * GDK])
        tmp_og = at("tmp_og", [P, 2, BLK], F32, gain_at)

        d = Region(arena, arena_end)
        qk_at = d.o
        q_d = d("dsa_q", [P, DH, SEQ])
        k_d = d("dsa_k", [P, DH, SEQ])
        qk_end = d.o
        v_at = d.o
        v_d = d("dsa_v", [P, TILES, D])
        gate_d = d("dsa_gate", [P, KT, TOK])
        v_end = d.o
        bias_p = [None] + [d(f"dsa_bias{t}", [P, P * (t + 1)]) for t in range(1, NP_T)]
        bias_s = d("dsa_bias_s", [NS, KEYS], BF16)
        ikw = d("dsa_ikw", [P, TILES, ID + IH])
        qs_d = d("dsa_q_s", [P, DH, NS])
        ks_d = d("dsa_k_s", [P, DH, NS])
        ast = d("dsa_ast", [P, 2, 4])
        w_stack = d("dsa_w_stack", [P, 1])
        w_sel = d("dsa_w_sel", [P, NS])
        top8 = d("dsa_top8", [P, 8])
        kst_at = d.o
        k_st = d("dsa_k_st", [P, TILES, BLK])
        kst_end = d.o
        dx = Region(xn_at, xn_end)
        score_s = dx("dsa_score_s", [NS, KEYS])
        tmp_d = dx("dsa_tmp", [P, BLK])
        tmp_d2 = dx("dsa_tmp2", [P, 8 * NS])
        i = Region(v_at, v_end)
        iq = i("idx_q", [ID, IH, TOK])
        iq_seq = i("idx_q_seq", [ID, IH, DB, NS])
        ik = i("idx_k", [ID + IH, TOK])
        ik_old = i("idx_k_old", [ID, 2, BLK])
        relu_p = i("idx_relu", [P, 2, BLK])
        relu_s = i("idx_relu_s", [P, KEYS])
        a = Region(kst_at, kst_end)
        s_at = a("att_s", [P, 2, BLK])
        p_at = a("att_p", [P, 2, BLK])
        pt_at = at("att_pt", [P, 2, BLK], F32, gain_at)
        o = Region(qk_at, qk_end)
        kt_s = o("smp_kt", [P, 2, DH, PAGE])
        q_heads = o("smp_q", [P, DH, DB, NS])
        p_s = o("smp_p", [P, KEYS])
        pt_s = o("smp_pt", [P, NPAGE, P])
        ptn_s = o("smp_ptn", [NS, P])

        p = Region(arena, arena_end)
        u_p = p("pool_u", [P, KT, PADW + SEQ])
        u_s = p("pool_u_s", [P, KT, DB, PADW + DQ])
        u_new = p("pool_u_new", [P, KT, NS])
        gate_p = p("pool_gate", [P, KT, TOK])
        d_hi = p("pool_d_hi", [P, KT, TOK], F32R)
        d_lo = p("pool_d_lo", [P, KT, TOK], F32R)
        px = Region(xn_at, xn_end)
        win = px("pool_win", [P, 2, PADW + SEQ])
        win_s = px("pool_win_s", [P, 2, DB, PADW + DQ])
        small_d = px("pool_small", [P, PADW])
        d_tmp = at("pool_d_tmp", [P, TOK], F32, gain_at)
        old_rows = p("pool_old", [DB * STATE, D])
        new_rows = p("pool_rows", [NS, 2, D])

        psum = ctx.enter_context(nc.psum_tensor("psum", [P, NBANK, 512], F32))
        wide = psum[:].rearrange("p b c -> p (b c)")

        items = []

        def f_item(key, w, c0, n, kk=KT):
            items.append((key, w[:, c0:c0 + n].rearrange("(k p) n -> p k n", p=P), kk, n, "w"))

        def t_item(key, w, c0, n, k0, kk):
            items.append((key, w[k0 * P:(k0 + kk) * P, c0:c0 + n].rearrange("(k p) n -> p k n", p=P), kk, n, "w"))

        def t_block(key, w, c0, n):
            for kh in range(2):
                t_item(key + (n, kh), w, c0 + n * BLK, BLK, kh * 4, 4)

        for L, kind in enumerate(KINDS):
            j = L // 3
            if kind == 0:
                w = gla_w_in[j]
                t_block((L, "v"), w, 2 * GH * GDK, 0)
                f_item((L, "a"), w, 2 * GH * GDK + 2 * D, RANK)
                t_block((L, "v"), w, 2 * GH * GDK, 1)
                for x in range(2):
                    f_item((L, "k", x), w, GH * GDK + x * HALF, HALF)
                for x in range(2):
                    f_item((L, "q", x), w, x * HALF, HALF)
                for x in range(4):
                    f_item((L, "g", x), w, 2 * GH * GDK + D + x * HALF, HALF)
                for n in range(2):
                    t_block((L, "out"), gla_w_out[j], 0, n)
            elif kind == 1:
                w = dsa_w_in[j]
                c_iq = 4 * D
                f_item((L, "ikw"), w, c_iq + IH * ID, ID + IH)
                f_item((L, "iq"), w, c_iq, IH * ID)
                for x in range(2):
                    items.append(((L, "idx", x), None, 4, 512, "idx"))
                t_block((L, "k"), w, D, 0)
                f_item((L, "q", 0), w, 0, HALF)
                t_block((L, "k"), w, D, 1)
                for x in range(1, 4):
                    f_item((L, "q", x), w, x * HALF, HALF)
                for n in range(2):
                    t_block((L, "v"), w, 2 * D, n)
                for x in range(4):
                    f_item((L, "g", x), w, 3 * D + x * HALF, HALF)
                for grp in range(2):
                    for kv in "KV":
                        for b in range(4 * grp, 4 * grp + 4):
                            for x in range(NPAGE // 2):
                                items.append(((L, kv, b, x), None, 2, D, kv))
                for n in range(2):
                    t_block((L, "out"), dsa_w_out[j], 0, n)
            else:
                w = pool_w_in[j]
                for x in range(4):
                    f_item((L, "u", x), w, x * HALF, HALF)
                for x in range(4):
                    f_item((L, "g", x), w, D + x * HALF, HALF)
                items.append(((L, "grp"), pool_w_grp[j].rearrange("g (k p) n -> p (g k) n", p=P), KT, HALF, "w"))
                for n in range(2):
                    t_block((L, "out"), pool_w_out[j], 0, n)
        index = {it[0]: n for n, it in enumerate(items)}
        weights = [it[0] for it in items if it[4] == "w"]
        pair_of = {key: n for n, key in enumerate(weights)}

        def raw_view(key):
            n = index[key]
            kk, w = items[n][2:4]
            return raw[:, n % RAW, 0:kk * w].rearrange("p (k n) -> p k n", k=kk)

        def pair_view(t, key):
            kk, w = items[index[key]][2:4]
            return t[:, pair_of[key] % 2, 0:kk * w].rearrange("p (k n) -> p k n", k=kk)

        block = ctx.enter_context(nc.Block())

        @block.sync
        def _(sp):
            sp.dma_start(ptab[:], page_table.rearrange("(a b) c -> a (b c)", a=1)).then_inc(*sig("page_table", n=16))
            for t in range(NP_T):
                sp.dma_start(X[:, t, :], x_prompt[0, t * P:(t + 1) * P, :]).then_inc(*sig(f"x_in{t}", n=16))
            sp.dma_start(X[0:NS, SMP, :], x_sample.rearrange("b q d -> (b q) d")).then_inc(*sig(f"x_in{SMP}", n=16))

            def norm_gain(L):
                src = [gla_norm[0], dsa_norm[0], pool_norm[0], gla_norm[1], final_norm][L]
                if L:
                    sp.wait_ge(*on("h_lo", (L - 1, "out"), SMP, 1))
                sp.dma_start(gain[:], src.partition_broadcast(P)).then_inc(*sig("gain", L, n=16))

            def small(L):
                j = L // 3
                if KINDS[L] == 0:
                    if j:
                        sp.wait_ge(*on("h_lo", (0, "out"), SMP, 1))
                    sp.dma_start(w_a2[:], gla_w_a2[j]).then_inc(*sig("gla_small", L, 0, n=16))
                    sp.dma_start(b_a[:], gla_b_a[j].rearrange("(h p) -> p h", p=P),
                                 allow_slow_non_contiguous=True).then_inc(*sig("gla_small", L, 1, n=16))
                    sp.dma_start(g_on[:], gla_out_norm[j].partition_broadcast(P)).then_inc(*sig("gla_small", L, n=16))
                if KINDS[L] == 2:
                    sp.dma_start(scale_p[:], pool_scale[j].rearrange("(k p) -> p k", p=P), allow_slow_non_contiguous=True)\
                        .then_inc(*sig("pool_small", n=16))
                    sp.wait_ge(*on("h_lo", (L - 1, "out"), SMP, 1))
                    sp.wait_ge(*on("stores_v", "all"))
                    sp.wait_ge(*on("stores_ik", "all"))
                    for t in range(TILES):
                        sp.wait_ge(*on(f"stores_k{t}", "all"))
                    sp.dma_start(old_rows[:], state_pool[j].rearrange("b r d -> (b r) d"))\
                        .then_inc(*sig("pool_old", n=16))

            def state_load(L, b):
                j = L // 3
                if b >= 3:
                    sp.wait_ge(*on(f"s_stored{b % 3}", L, b - 3))
                elif L:
                    sp.wait_ge(*on("h_lo", (L - 1, "out"), SMP, 1))
                sp.dma_start(s_in[:, b % 3], state_gla[j, b].rearrange("h k v -> k h v"))\
                    .then_inc(*sig(f"s_in{b % 3}", L, b, n=16))

            norm_gain(0)
            small(0)
            small_done = {0}
            page = {}
            sp.wait_ge(*on("page_table"))
            for n, (key, src, kk, w, kind) in enumerate(items):
                L = key[0]
                if n >= RAW:
                    old = items[n - RAW]
                    if old[4] == "w":
                        sp.wait_ge(*on("split", old[0]))
                    else:
                        sp.wait_ge(*on("pages_used", old[0]))
                s = n % RAW
                if kind == "w":
                    sp.dma_start(raw_view(key), src).then_inc(*sig(f"raw{s}", key, n=16))
                elif kind == "idx":
                    for b in range(4):
                        for pg in range(NPAGE):
                            col = (key[2] * 4 + b) * NPAGE + pg
                            r = sp.value_load(ptab[0:1, col:col + 1], min_val=0, max_val=cache_k.shape[1] - 1)
                            sp.dma_start(raw[:, s, (b * NPAGE + pg) * ID:(b * NPAGE + pg + 1) * ID],
                                         cache_idx_k[0, bass.ds(r, 1)].rearrange("a p n -> (a p) n"))\
                                .then_inc(*sig(f"raw{s}", key, n=16))
                else:
                    cache = cache_k if kind == "K" else cache_v
                    for x in range(2):
                        col = key[2] * NPAGE + key[3] * 2 + x
                        r = sp.value_load(ptab[0:1, col:col + 1], min_val=0, max_val=cache_k.shape[1] - 1)
                        sp.dma_start(raw[:, s, x * D:(x + 1) * D],
                                     cache[0, bass.ds(r, 1)].rearrange("a p h e -> (a p) (h e)"))\
                            .then_inc(*sig(f"raw{s}", key, n=16))
                if key == (L, "g", 3) and KINDS[L] == 0:
                    for b in range(3):
                        state_load(L, b)
                if key == (L, "out", 0, 1) and KINDS[L] == 0:
                    for b in range(3, DB):
                        state_load(L, b)
                if key == (L, "out", 1, 1):
                    norm_gain(L + 1)
                    if L + 1 < len(KINDS):
                        small(L + 1)
            for name in ("stores_pool", "stores_v", "stores_ik", "stores_gla", "stores_y0", "stores_y1"):
                sp.wait_ge(*on(name, "all"))
            for t in range(TILES):
                sp.wait_ge(*on(f"stores_k{t}", "all"))
            for s in range(3):
                sp.wait_ge(*on(f"s_stored{s}", "all"))

        @block.gpsimd
        def _(pool):
            def select(out, fill, base, pattern, mult, op=ALU.is_ge):
                pool.affine_select(out=out, in_=out, compare_op=op, fill=fill, base=base, pattern=pattern,
                                   channel_multiplier=mult).then_inc(*sig("const"))
                pool.wait_ge(*on_now("const"))

            def fill(out, value):
                pool.memset(out, value).then_inc(*sig("const"))
                pool.wait_ge(*on_now("const"))

            def on_now(name):
                return semaphore(name), count[name]

            fill(ident[:], 0.0)
            select(ident[:], 1.0, 0, [[-1, P]], 1, ALU.not_equal)
            fill(eps[:], RMS_EPS)
            fill(one[:], 1.0)
            plan.value[("const", "first")] = count["const"]

            def other_constants():
                fill(no_reset[:], 1.0)
                fill(no_reset[:, 0:SEQ:CH], 0.0)
                fill(no_reset[:, SEQ:TOK:DQ], 0.0)
                fill(chunk_tri[:], 1.0)
                select(chunk_tri[:], 0.0, 0, [[1, P]], -1)
                fill(chunk_tri[0:CH, CH:P], 0.0)
                fill(seq_tri[:], 1.0)
                select(seq_tri[:], 0.0, 0, [[1, NS]], -1)
                sv = seq_tri[:].rearrange("p (b q) -> p b q", b=DB)
                select(sv, 0.0, 0, [[-DQ, DB], [0, DQ]], 1)
                fill(future_p[:], 0.0)
                select(future_p[:], FUTURE, 0, [[-1, P]], 1)
                fill(future_s[:], 0.0)
                select(future_s[:], FUTURE, 0, [[-1, NS]], 1)
                fv = future_s[:].rearrange("p (b q) -> p b q", b=DB)
                select(fv, FUTURE, DQ - 1, [[DQ, DB], [0, DQ]], -1)
                fill(stack4[:], 0.0)
                for h in range(IH):
                    select(stack4[:], 1.0, -NS * h, [[-1, NS]], 1, ALU.not_equal)
                fill(pick_tok[:], 0.0)
                pv = pick_tok[:].rearrange("p b (h q) -> p b h q", q=DQ)
                select(pv, 1.0, 0, [[-DQ, DB], [0, DH], [-1, DQ]], 1, ALU.not_equal)
                fill(seq_col[:], 1.0)
                select(seq_col[:], 0.0, 0, [[-DQ, DB], [1, NS]], 0)
                select(seq_col[:], 0.0, DQ - 1, [[DQ, DB], [-1, NS]], 0)
                fill(seq_row[:], 1.0)
                select(seq_row[:], 0.0, 0, [[-DQ, DB]], 1)
                select(seq_row[:], 0.0, DQ - 1, [[DQ, DB]], -1)
                pool.iota(cnt_i[:].bitcast(I32), pattern=[[1, PADW]], base=1, channel_multiplier=0)\
                    .then_inc(*sig("const"))
                pool.wait_ge(*on_now("const"))
                pool.tensor_copy(inv_cnt[:], cnt_i[:].bitcast(I32)).then_inc(*sig("const"))

            for n, key in enumerate(weights):
                if n == 2:
                    other_constants()
                s = index[key] % RAW
                pool.wait_ge(*on(f"raw{s}", key))
                if n >= 2:
                    pool.wait_ge(*on("proj", ("item", weights[n - 2])))
                pool.tensor_tensor(pair_view(w_hi, key), raw_view(key), one[:].unsqueeze(1).broadcast_to(
                    [P, *raw_view(key).shape[1:]]), ALU.mult)\
                    .then_inc(*sig("split_hi", key))
                pool.wait_ge(*on("split_hi", key))
                pool.tensor_tensor(pair_view(w_lo, key), raw_view(key), pair_view(w_hi, key).bitcast(F32),
                                   ALU.subtract).then_inc(*sig("split", key))

        @block.tensor
        def _(pe):
            reader = {}

            def claim(b, key, last):
                if b in reader:
                    pe.wait_ge(*on(*reader[b]))
                reader[b] = last
                plan.bank[key] = b
                return b

            turn = {"n": 0}

            def next_bank(banks=range(NBANK)):
                turn["n"] += 1
                return banks[turn["n"] % len(banks)]

            def product(out, lh, ll, rh, rl, start, stop):
                pe.matmul(out, lh, rh, start=start, stop=False)
                pe.matmul(out, lh, rl, start=False, stop=False)
                return pe.matmul(out, ll, rh, start=False, stop=stop)

            def norm_in(L):
                for t in range(TILES):
                    pe.wait_ge(*on("xn", L, t))
                    for half in range(2):
                        b = claim(next_bank(), ("nT", L, t, half), ("h_lo", L, t, half))
                        for k in range(4):
                            mm = pe.transpose(psum[:, b, k * P:k * P + rows(t)],
                                              xn[0:rows(t), t % 2, (4 * half + k) * P:(4 * half + k + 1) * P],
                                              ident[0:rows(t), 0:rows(t)])
                        mm.then_inc(*sig("nT", L, t, half))

            def wait_h(tag):
                for t in range(TILES):
                    pe.wait_ge(*on("h_lo", tag, t, 1))

            def part_job(name, m, reader_name, banks, lhs, rhs, kk, items_done=()):
                for part, c in PARTS:
                    b = claim(banks[part] if len(banks) == 2 else next_bank(banks), ("proj", name, part),
                              (reader_name, name, part))
                    for k in range(kk):
                        mm = product(psum[0:m, b, 0:HC], *lhs(k), *rhs(k, c), k == 0, k == kk - 1)
                    mm.then_inc(*sig("proj", name, part, also=items_done if part else ()))

            def h_pair(k, c):
                return h_hi[:, k, c], h_lo[:, k, c]

            def f_job(key, jobs, reader_name, banks):
                wh, wl = pair_view(w_hi, key), pair_view(w_lo, key)
                pe.wait_ge(*on("split", key))
                for x, (name, c0, m) in enumerate(jobs):
                    part_job(name, m, reader_name, banks, lambda k: (wh[:, k, c0:c0 + m], wl[:, k, c0:c0 + m]),
                             h_pair, KT, ((("item", key),),) if x == len(jobs) - 1 else ())

            def t_job(keys, name, n, reader_name, banks, tag):
                bs, k0 = [], 0
                for x, key in enumerate(keys):
                    wh, wl = pair_view(w_hi, key), pair_view(w_lo, key)
                    kk = items[index[key]][2]
                    pe.wait_ge(*on("split", key))
                    for t in range(TILES):
                        if x == 0:
                            pe.wait_ge(*on("h_lo", tag, t, 1))
                            bs.append(claim(next_bank(banks), ("proj", name, t), (reader_name, name, t)))
                        for k in range(kk):
                            mm = product(psum[0:rows(t), bs[t], 0:n], h_hi[:, k0 + k, cols(t)],
                                         h_lo[:, k0 + k, cols(t)], wh[:, k, :], wl[:, k, :],
                                         k0 + k == 0, k0 + k == KT - 1)
                        last_t = ((("item", key),),) if t == TILES - 1 else ()
                        if x == len(keys) - 1:
                            mm.then_inc(*sig("proj", (name, t), also=last_t))
                        elif t == TILES - 1:
                            mm.then_inc(*sig("proj", ("item", key)))
                    k0 += kk

            def out_proj(L):
                for n in range(2):
                    t_job([(L, "out", n, kh) for kh in range(2)], (L, "out", n), BLK, "resid", range(NBANK),
                          (L, "out"))

            def out_transposes(L, t, source, ready):
                pe.wait_ge(*on(*ready))
                for half in range(2):
                    b = claim(next_bank(), ("oT", L, t, half), ("oT_read", L, t, half))
                    for k in range(4):
                        kt = 4 * half + k
                        mm = pe.transpose(psum[:, b, k * P:k * P + rows(t)],
                                          source[0:rows(t), t, kt * P:(kt + 1) * P], ident[0:rows(t), 0:rows(t)])
                    mm.then_inc(*sig("oT", L, t, half))

            def gla(L):
                norm_in(L)
                t_job([(L, "v", 0, kh) for kh in range(2)], (L, "v", 0), BLK, "v", range(NBANK), L)
                f_job((L, "a"), [((L, "a"), 0, RANK)], "a", range(NBANK))
                pe.wait_ge(*on("a", (L, "a"), 1))
                pe.wait_ge(*on("gla_small", L))
                bs = claim(next_bank(), ("z", L, "s"), ("z_read", L, "s"))
                for h in range(GH):
                    b = claim(next_bank(), ("z", L, h), ("z_read", L, h))
                    w = w_a2[:, h * GDK:(h + 1) * GDK]
                    pe.matmul(psum[:, b, 0:SEQ], w, a_t[:, 0:SEQ], start=True, stop=True).then_inc(*sig("z", L, h))
                    mm = pe.matmul(psum[:, bs, h * NS:(h + 1) * NS], w, a_t[:, SEQ:TOK], start=True, stop=True)
                mm.then_inc(*sig("z", L, "s"))
                t_job([(L, "v", 1, kh) for kh in range(2)], (L, "v", 1), BLK, "v", range(NBANK), L)
                for x in range(2):
                    f_job((L, "k", x), [((L, "k", 2 * x + y), y * P, P) for y in range(2)], "k_gated", range(NBANK))
                for x in range(2):
                    f_job((L, "q", x), [((L, "q", 2 * x + y), y * P, P) for y in range(2)], "q_gated", range(NBANK))
                pe.wait_ge(*on("k_gated", (L, "k", GH - 1), 1))
                for t in range(TILES):
                    b = claim(next_bank(), ("kT", L, t), ("k_tok", L, t))
                    for h in range(GH):
                        mm = pe.transpose(psum[0:rows(t), b, h * P:(h + 1) * P], kg[:, h, cols(t)], ident[:])
                    mm.then_inc(*sig("kT", L, t))
                pe.wait_ge(*on("q_gated", (L, "q", GH - 1), 1))
                pe.wait_ge(*on("v", (L, "v", 1), SMP))

                def states(c):
                    r = slice((c % 2) * CH, (c % 2) * CH + CH)
                    for half in range(2):
                        claim(1 + half, ("state", L, c, half), ("s_sum", L, c))
                    for h in range(GH):
                        mm = pe.matmul(psum[:, 1 + h // 2, (h % 2) * GDV:(h % 2 + 1) * GDV],
                                       k_tok[r, c // 2, h * GDK:(h + 1) * GDK],
                                       v_g[r, c // 2, h * GDV:(h + 1) * GDV], start=True, stop=True)
                    mm.then_inc(*sig("state", L, c))

                def carried(c, last):
                    r = (c % 2) * CH
                    if c:
                        pe.wait_ge(*on("s_now", L, c))
                    for h in range(GH):
                        if c:
                            mm = pe.matmul(psum[r:r + CH, 3 + h // 2, (h % 2) * GDV:(h % 2 + 1) * GDV],
                                           qg[:, h, c * CH:(c + 1) * CH], s_now[:, c % 2, h * GDV:(h + 1) * GDV],
                                           start=False, stop=last and h % 2 == 1, skip_group_check=True)
                    if last:
                        mm.then_inc(*sig("o", L, c // 2))

                g_jobs = [((L, "g", 2 * x + y), (L, "g", x), y) for x in range(4) for y in range(2)]

                def g_job(n):
                    name, key, y = g_jobs[n]
                    if y == 0:
                        pe.wait_ge(*on("split", key))
                    wh, wl = pair_view(w_hi, key), pair_view(w_lo, key)
                    part_job(name, P, "gate", ((5, 6)[n % 2], 7),
                             lambda k: (wh[:, k, y * P:(y + 1) * P], wl[:, k, y * P:(y + 1) * P]), h_pair, KT,
                             ((("item", key),),) if y else ())

                for t in range(NP_T):
                    claim(0, ("att", L, t), ("att_m", L, t))
                    for h in range(GH):
                        mm = pe.matmul(psum[:, 0, h * P:(h + 1) * P], kg[:, h, cols(t)], qg[:, h, cols(t)],
                                       start=True, stop=True)
                    mm.then_inc(*sig("att", L, t))
                    pe.wait_ge(*on("k_tok", L, t))
                    states(2 * t)
                    g_job(2 * t)
                    pe.wait_ge(*on("att_m", L, t))
                    for half in range(2):
                        claim(3 + half, ("o", L, t, half), ("o_out", L, t))
                    for h in range(GH):
                        pe.matmul(psum[:, 3 + h // 2, (h % 2) * GDV:(h % 2 + 1) * GDV], att_g[:, h, :],
                                  v_g[:, t, h * GDV:(h + 1) * GDV], start=h % 2 == 0, stop=False,
                                  skip_group_check=True)
                    carried(2 * t, False)
                    states(2 * t + 1)
                    g_job(2 * t + 1)
                    carried(2 * t + 1, True)

                claim(0, ("att", L, SMP), ("att_m", L, SMP))
                for h in range(GH):
                    mm = pe.matmul(psum[0:NS, 0, h * NS:(h + 1) * NS], kg[:, h, SEQ:TOK], qg[:, h, SEQ:TOK],
                                   start=True, stop=True)
                mm.then_inc(*sig("att", L, SMP))
                pe.wait_ge(*on("att_m", L, SMP))
                for half in range(2):
                    claim(3 + half, ("o", L, SMP, half), ("o_out", L, SMP))
                for h in range(GH):
                    pe.matmul(psum[0:NS, 3 + h // 2, (h % 2) * GDV:(h % 2 + 1) * GDV], att_g[0:NS, h, 0:NS],
                              v_g[0:NS, SMP, h * GDV:(h + 1) * GDV], start=h % 2 == 0, stop=False,
                              skip_group_check=True)
                pe.wait_ge(*on("q_seq", L))
                for b in range(DB):
                    pe.wait_ge(*on(f"s_in{b % 3}", L, b))
                    for h in range(GH):
                        mm = pe.matmul(psum[0:NS, 3 + h // 2, (h % 2) * GDV:(h % 2 + 1) * GDV],
                                       q_seq[:, h, b, :], s_in[:, b % 3, h, :], start=False,
                                       stop=b == DB - 1 and h % 2 == 1, skip_group_check=True)
                    if b == DB - 1:
                        mm.then_inc(*sig("o", L, SMP))
                    pe.wait_ge(*on("k_seq", L, b))
                    pair = (1, 2) if b % 2 else (5, 6)
                    for half in range(2):
                        claim(pair[half], ("s_state", L, b, half), ("s_new", L, b))
                    for h in range(GH):
                        mm = pe.matmul(psum[:, pair[h // 2], (h % 2) * GDV:(h % 2 + 1) * GDV],
                                       k_seq[:, b % 2, h * GDK:(h + 1) * GDK],
                                       v_g[0:NS, SMP, h * GDV:(h + 1) * GDV], start=True, stop=True)
                    mm.then_inc(*sig("s_state", L, b))
                for t in range(TILES):
                    out_transposes(L, t, v_g, ("o_norm", L, t))
                out_proj(L)

            def dsa(L):
                norm_in(L)
                wait_h(L)
                f_job((L, "ikw"), [((L, "ikw"), 0, ID + IH)], "ik", range(NBANK))
                f_job((L, "iq"), [((L, "iq", y), y * P, P) for y in range(2)], "iq", range(NBANK))
                pe.wait_ge(*on("ik", (L, "ikw"), 1))
                for x, tiles in enumerate((range(NP_T), (SMP,))):
                    b = claim(next_bank(), ("ikwT", L, x), ("ikw", L, x))
                    for t in tiles:
                        mm = pe.transpose(psum[0:rows(t), b, (t % 4) * P:(t % 4) * P + ID + IH], ik[:, cols(t)],
                                          ident[0:ID + IH, 0:ID + IH])
                    mm.then_inc(*sig("ikwT", L, x))
                pe.wait_ge(*on("iq", (L, "iq", 1), 1))
                for t in range(1, NP_T):
                    for h in range(IH):
                        b = claim(next_bank(), ("idx", L, t, h), ("idx_relu", L, t, h))
                        pe.matmul(psum[:, b, 0:(t + 1) * P], iq[:, h, cols(t)], ik[0:ID, 0:(t + 1) * P],
                                  start=True, stop=True).then_inc(*sig("idx", L, t, h))
                pe.wait_ge(*on("iq_seq", L))
                for c in range(2):
                    claim(c, ("idx_s", L, c), ("idx_relu_s", L, c))
                    for b in range(DB):
                        if b % 4 == 0:
                            key = (L, "idx", b // 4)
                            pe.wait_ge(*on(f"raw{index[key] % RAW}", key))
                        key = (L, "idx", b // 4)
                        kb = claim((3, 4)[b % 2], ("oldT", L, c, b), ("ik_old", L, c, b))
                        for pg in range(4):
                            o = ((b % 4) * NPAGE + 4 * c + pg) * ID
                            mm = pe.transpose(psum[0:ID, kb, pg * P:(pg + 1) * P],
                                              raw[:, index[key] % RAW, o:o + ID], ident[:])
                        mm.then_inc(*sig("pages_used", L, c, b,
                                         also=((key,),) if c == 1 and b % 4 == 3 else ()))
                        pe.wait_ge(*on("ik_old", L, c, b))
                        for h in range(IH):
                            mm = pe.matmul(psum[h * NS:(h + 1) * NS, c, :], iq_seq[:, h, b, :], ik_old[:, b % 2, :],
                                           start=b == 0, stop=b == DB - 1)
                        mm.then_inc(*sig("idx_s", L, c, b, also=(((L, c),) if b == DB - 1 else ())))
                claim(2, ("idx_s", L, 2), ("idx_relu_s", L, 2))
                for h in range(IH):
                    mm = pe.matmul(psum[h * NS:(h + 1) * NS, 2, 0:NS], iq[:, h, SEQ:TOK], ik[0:ID, SEQ:TOK],
                                   start=True, stop=True)
                mm.then_inc(*sig("idx_s", L, 2))
                pe.wait_ge(*on("w_sel", L))
                for c, w in enumerate((BLK, BLK, NS)):
                    pe.wait_ge(*on("idx_relu_s", L, c))
                    b = claim(5 + c, ("score_s", L, c), ("score_s", L, c))
                    pe.matmul(psum[0:NS, b, 0:w], w_sel[:], relu_s[:, c * BLK:c * BLK + w], start=True, stop=True)\
                        .then_inc(*sig("score_mm", L, c))

                def k_transposes(n):
                    for t in range(TILES):
                        pe.wait_ge(*on("k_st", (L, "k", n), t))
                        b = claim(next_bank(), ("dkT", L, n, t), ("k_d", L, n, t))
                        for h in range(4):
                            mm = pe.transpose(psum[:, b, h * P:h * P + rows(t)], k_st[0:rows(t), t, h * P:(h + 1) * P],
                                              ident[0:rows(t), 0:rows(t)])
                        mm.then_inc(*sig("dkT", L, n, t))

                t_job([(L, "k", 0, kh) for kh in range(2)], (L, "k", 0), BLK, "k_st", range(NBANK), L)
                f_job((L, "q", 0), [((L, "q", y), y * P, P) for y in range(2)], "q_d", range(NBANK))
                k_transposes(0)
                t_job([(L, "k", 1, kh) for kh in range(2)], (L, "k", 1), BLK, "k_st", range(NBANK), L)
                for x in range(1, 4):
                    f_job((L, "q", x), [((L, "q", 2 * x + y), y * P, P) for y in range(2)], "q_d", range(NBANK))
                    if x == 1:
                        k_transposes(1)
                for n in range(2):
                    t_job([(L, "v", n, kh) for kh in range(2)], (L, "v", n), BLK, "v_d", range(NBANK), L)
                for x in range(4):
                    f_job((L, "g", x), [((L, "g", 2 * x + y), y * P, P) for y in range(2)], "gate", range(NBANK))

                pe.wait_ge(*on("q_d", (L, "q", DH - 1), 1))
                pe.wait_ge(*on("k_d", L, 1, SMP))
                pe.wait_ge(*on("v_d", (L, "v", 1), SMP))
                units = [(t, h) for t in range(NP_T) for h in range(DH)]

                def scores(n):
                    t, h = units[n]
                    b = claim((0, 1)[n % 2], ("S", L, n), ("S_read", L, n))
                    pe.matmul(psum[:, b, 0:(t + 1) * P], q_d[:, h, cols(t)], k_d[:, h, 0:(t + 1) * P],
                              start=True, stop=True).then_inc(*sig("S", L, n))

                def probs(n):
                    t, h = units[n]
                    b = claim((2, 3)[n % 2], ("PT", L, n), ("PT_read", L, n))
                    pe.wait_ge(*on("p_norm", L, n))
                    for s in range(t + 1):
                        mm = pe.transpose(psum[:, b, s * P:(s + 1) * P], p_at[:, n % 2, s * P:(s + 1) * P], ident[:])
                    mm.then_inc(*sig("PT", L, n))

                def values(n):
                    t, h = units[n]
                    m = n // 4
                    if n % 4 == 0:
                        claim((4, 5)[m % 2], ("O", L, m), ("oT_read", L, t, h // 4))
                    b = (4, 5)[m % 2]
                    pe.wait_ge(*on("PT_read", L, n))
                    for s in range(t + 1):
                        mm = pe.matmul(psum[:, b, (h % 4) * P:(h % 4 + 1) * P], v_d[:, s, h * HD:(h + 1) * HD],
                                       pt_at[:, n % 2, s * P:(s + 1) * P], start=s == 0, stop=s == t)
                    mm.then_inc(*sig("O", L, n))

                N = len(units)
                for n in range(N + 2):
                    if n < N:
                        scores(n)
                    if 1 <= n <= N:
                        probs(n - 1)
                    if n >= 2:
                        values(n - 2)

                pe.wait_ge(*on("bias_s", L))
                for grp in range(2):
                    for x in range(3):
                        claim(x, ("SS", L, grp, x), ("ss_read", L, grp))
                    for bl in range(4):
                        b = 4 * grp + bl
                        r = slice(bl * NS, (bl + 1) * NS)
                        for pg in range(NPAGE):
                            key = (L, "K", b, pg // 2)
                            s = index[key] % RAW
                            if pg % 2 == 0:
                                pe.wait_ge(*on(f"raw{s}", key))
                            turn_s = (b * NPAGE + pg) % 2
                            for half in range(2):
                                kb = claim(4 + 2 * turn_s + half, ("KT", L, b, pg, half), (f"kt_s{half}", L, b, pg))
                                for h in range(4):
                                    o = (pg % 2) * D + (4 * half + h) * HD
                                    mm = pe.transpose(psum[:, kb, h * P:(h + 1) * P], raw[:, s, o:o + HD], ident[:])
                                mm.then_inc(*sig("pages_used", L, "kT", b, pg, half,
                                                 also=((key,),) if pg % 2 and half else ()))
                            c = pg * PAGE
                            out = psum[r, c // BLK, c % BLK:c % BLK + PAGE]
                            pe.matmul(out, pick_tok[:, b, :], bias_s[:, c:c + PAGE], start=True, stop=False)
                            if b == 0 and pg == 0:
                                pe.wait_ge(*on("q_heads", L))
                            for half in range(2):
                                pe.wait_ge(*on(f"kt_s{half}", L, b, pg))
                                for h in range(4 * half, 4 * half + 4):
                                    mm = pe.matmul(out, q_heads[:, h, b, :], kt_s[:, turn_s, h, :], start=False,
                                                   stop=h == DH - 1)
                            mm.then_inc(*sig("SS_page", L, b, pg))
                        out = psum[r, 2, 0:NS]
                        pe.matmul(out, pick_tok[:, b, :], bias_s[:, PAST:KEYS], start=True, stop=False)
                        for h in range(DH):
                            mm = pe.matmul(out, q_heads[:, h, b, :], ks_d[:, h, :], start=False, stop=h == DH - 1)
                    mm.then_inc(*sig("SS", L, grp))
                    pe.wait_ge(*on("ps_norm", L, grp))
                    for x in range(3):
                        b = claim(4 + x, ("PsT", L, grp, x), ("pt_s", L, grp, x))
                        if x < 2:
                            for pg in range(4):
                                o = (4 * x + pg) * PAGE
                                mm = pe.transpose(psum[:, b, pg * P:(pg + 1) * P], p_s[:, o:o + PAGE], ident[:])
                        else:
                            mm = pe.transpose(psum[0:NS, b, 0:P], p_s[:, PAST:KEYS], ident[:])
                        mm.then_inc(*sig("PsT", L, grp, x))
                    pe.wait_ge(*on("pt_s", L, grp, 2))
                    if grp == 0:
                        claim(3, ("Os",), ("os_read", L))
                    o_s = psum[:, 3, 0:DH * NS].rearrange("p (h t) -> p h t", h=DH)
                    for bl in range(4):
                        b = 4 * grp + bl
                        for pg in range(NPAGE):
                            key = (L, "V", b, pg // 2)
                            s = index[key] % RAW
                            if pg % 2 == 0:
                                pe.wait_ge(*on(f"raw{s}", key))
                            for h in range(DH):
                                o = (pg % 2) * D + h * HD
                                c = bl * NS + h * DQ
                                mm = pe.matmul(o_s[:, h, b * DQ:(b + 1) * DQ], raw[:, s, o:o + HD],
                                               pt_s[:, pg, c:c + DQ], start=pg == 0 and h == 0, stop=False,
                                               skip_group_check=True)
                            if pg % 2:
                                mm.then_inc(*sig("pages_used", key))
                        for h in range(DH):
                            c = bl * NS + h * DQ
                            mm = pe.matmul(o_s[:, h, b * DQ:(b + 1) * DQ], v_d[0:NS, SMP, h * HD:(h + 1) * HD],
                                           ptn_s[:, c:c + DQ], start=False, stop=h == DH - 1,
                                           skip_group_check=True)
                    mm.then_inc(*sig("Os", L, grp))
                out_proj(L)

            def pooling(L):
                norm_in(L)
                wait_h(L)
                for x in range(4):
                    f_job((L, "u", x), [((L, "u", 2 * x + y), y * P, P) for y in range(2)], "u", range(NBANK))
                pe.wait_ge(*on("pool_old"))
                for half in range(2):
                    b = claim(next_bank(), ("oldP", L, half), ("u_old", L, half))
                    for k in range(4):
                        mm = pe.transpose(psum[:, b, k * P:k * P + DB * STATE],
                                          old_rows[:, (4 * half + k) * P:(4 * half + k + 1) * P],
                                          ident[0:DB * STATE, 0:DB * STATE])
                    mm.then_inc(*sig("oldP", L, half))
                for x in range(4):
                    f_job((L, "g", x), [((L, "g", 2 * x + y), y * P, P) for y in range(2)], "gate", range(NBANK))
                pe.wait_ge(*on("u", (L, "u", KT - 1), 1))
                for part, m in ((0, STATE), (1, NS)):
                    for half in range(2):
                        b = claim(next_bank(), ("rowsT", L, part, half), ("pool_rows", L, part, half))
                        for k in range(4):
                            kt = 4 * half + k
                            src = u_p[:, kt, PADW + SEQ - STATE:] if part == 0 else u_new[:, kt, :]
                            mm = pe.transpose(psum[0:m, b, k * P:(k + 1) * P], src, ident[:])
                        mm.then_inc(*sig("rowsT", L, part, half))
                key = (L, "grp")
                pe.wait_ge(*on("split", key))
                wh, wl = pair_view(w_hi, key), pair_view(w_lo, key)
                for grp in range(len(WINDOWS)):
                    pe.wait_ge(*on("d_lo", L, 2 * grp + 1))
                    for y in range(2):
                        name = (L, "y", 2 * grp + y)
                        part_job(name, P, "y_read", range(NBANK),
                                 lambda k: (wh[:, 2 * grp + k, y * P:(y + 1) * P],
                                            wl[:, 2 * grp + k, y * P:(y + 1) * P]),
                                 lambda k, c: (d_hi[:, 2 * grp + k, c], d_lo[:, 2 * grp + k, c]), 2,
                                 ((("item", key),),) if grp == 3 and y else ())
                out_proj(L)

            pe.wait_ge(*on("const", "first"))
            for L, kind in enumerate(KINDS):
                (gla, dsa, pooling)[kind](L)

        @block.scalar
        def _(act):
            def copy(out, in_, scale=1.0):
                return act.activation(out, in_, ACT.Copy, scale=scale)

            def rstd_guess(sq, ln, y, n_inv, key):
                act.activation(ln, sq, ACT.Ln, bias=eps[0:ln.shape[0], :], scale=n_inv).then_inc(*sig("rstd_ln", *key))
                act.wait_ge(*on("rstd_ln", *key))
                act.activation(y, ln, ACT.Exp, scale=-0.5).then_inc(*sig("rstd_y", *key))

            def norm_hi(L, t):
                r = rows(t)
                for half in range(2):
                    act.wait_ge(*on("nT", L, t, half))
                    b = bank_of("nT", L, t, half)
                    copy(h_hi[:, 4 * half:4 * half + 4, cols(t)],
                         psum[:, b, :].rearrange("p (k t) -> p k t", k=4)[:, :, 0:r])\
                        .then_inc(*sig("h_hi", L, t, half))

            def norm(L, last=False):
                for t in range(TILES):
                    r = rows(t)
                    if L:
                        act.wait_ge(*on("resid", (L - 1, "out", 1), t))
                    else:
                        act.wait_ge(*on(f"x_in{t}"))
                    if t >= 2:
                        act.wait_ge(*on("xn", L, t - 2))
                    s = st[0:r, t % 2, :]
                    act.activation(sq_junk[0:r, :], X[0:r, t, :], ACT.Square, accum_out=s[:, 0:1])\
                        .then_inc(*sig("sumsq", L, t))
                    act.wait_ge(*on("sumsq", L, t))
                    rstd_guess(s[:, 0:1], s[:, 2:3], s[:, 3:4], 1.0 / D, (L, t))
                    if t and not last:
                        norm_hi(L, t - 1)
                    if last:
                        act.wait_ge(*on("xn", L, t))
                        dst = y_prompt[0, t * P:(t + 1) * P, :] if t < NP_T else y_sample.rearrange("b q d -> (b q) d")
                        act.dma_start(dst, xn[0:r, t % 2, :]).then_inc(*sig(f"stores_y{t % 2}", t, n=16))
                if not last:
                    norm_hi(L, SMP)

            def out_hi(L, t, half):
                act.wait_ge(*on("oT_read", L, t, half))
                n = rows(t)
                copy(h_hi[:, 4 * half:4 * half + 4, cols(t)],
                     tmp_og[:, half, 0:4 * n].rearrange("p (k t) -> p k t", k=4))\
                    .then_inc(*sig("h_hi", (L, "out"), t, half))

            def f_out(name, out, mark, fn=ACT.Copy, sample=None):
                m = out.shape[0]
                pieces = [(0, slice(0, HC), out[:, 0:HC])]
                if sample is None:
                    pieces += [(1, slice(0, HC), out[:, HC:TOK])]
                else:
                    pieces += [(1, slice(0, SEQ - HC), out[:, HC:SEQ]), (1, slice(SEQ - HC, HC), sample)]
                for part, c, dst in pieces:
                    act.wait_ge(*on("proj", name, part))
                    act.activation(dst, psum[0:m, bank_of("proj", name, part), c], fn).then_inc(*sig(mark, name, part))

            def t_out(name, t, out, mark):
                act.wait_ge(*on("proj", (name, t)))
                copy(out, psum[0:rows(t), bank_of("proj", name, t), 0:out.shape[-1]]).then_inc(*sig(mark, name, t))

            def gate(L, buf, k):
                f_out((L, "g", k), buf[:, k, :], "gate", ACT.Silu)

            def gla(L):
                j = L // 3
                norm(L)
                if L:
                    act.wait_ge(*on("stores_pool", "all"))
                for t in range(TILES):
                    t_out((L, "v", 0), t, v_g[0:rows(t), t, 0:BLK], "v")
                f_out((L, "a"), a_t[:], "a")
                act.wait_ge(*on("gla_small", L))
                for h in range(GH):
                    act.wait_ge(*on("z", L, h))
                    act.activation(soft[:, h, 0:SEQ], psum[:, bank_of("z", L, h), :], ACT.Abs,
                                   bias=b_a[:, h:h + 1]).then_inc(*sig("z_abs", L, h))
                act.wait_ge(*on("z", L, "s"))
                for h in range(GH):
                    act.activation(soft[:, h, SEQ:TOK], psum[:, bank_of("z", L, "s"), h * NS:(h + 1) * NS], ACT.Abs,
                                   bias=b_a[:, h:h + 1]).then_inc(*sig("z_abs", L, "s"))
                act.wait_ge(*on("z_abs", L, "s"))
                act.activation(soft[:], soft[:], ACT.Exp, scale=-1.0).then_inc(*sig("z_exp", L))
                act.wait_ge(*on("z_exp", L))
                act.activation(soft[:], soft[:], ACT.Ln, bias=one[:]).then_inc(*sig("z_soft", L))
                act.wait_ge(*on("decay", L))
                act.activation(kg[:], qg[:], ACT.Exp, scale=-1.0 / TAU).then_inc(*sig("k_decay", L))
                act.wait_ge(*on("k_decay", L))
                act.activation(qg[:], qg[:], ACT.Exp, scale=1.0 / TAU).then_inc(*sig("q_decay", L))
                act.wait_ge(*on("fac", L))
                act.activation(fac[:], fac[:], ACT.Exp, scale=1.0 / TAU).then_inc(*sig("fac_exp", L))
                for t in range(TILES):
                    t_out((L, "v", 1), t, v_g[0:rows(t), t, BLK:D], "v")
                for t in range(TILES):
                    act.wait_ge(*on("kT", L, t))
                    copy(k_tok[0:rows(t), t, :], psum[0:rows(t), bank_of("kT", L, t), :]).then_inc(*sig("k_tok", L, t))
                act.wait_ge(*on("fac_exp", L))

                def next_state(c):
                    act.wait_ge(*on("s_sum", L, c - 1))
                    if c % 2 and c > 1:
                        act.wait_ge(*on("o", L, c // 2 - 1))
                    for h in range(GH):
                        copy(s_now[:, c % 2, h * GDV:(h + 1) * GDV], s_sum[:, h * GDV:(h + 1) * GDV],
                             fac[:, h, c - 1:c]).then_inc(*sig("s_now", L, c))

                def squares(t):
                    r = rows(t)
                    act.wait_ge(*on("o_out", L, t))
                    if t:
                        act.wait_ge(*on("o_sq", L, t - 1))
                    for h in range(GH):
                        act.activation(sq_junk[0:r, h * GDV:(h + 1) * GDV], v_g[0:r, t, h * GDV:(h + 1) * GDV], ACT.Square,
                                       accum_out=ost[0:r, 0, 4 * t + h:4 * t + h + 1])\
                            .then_inc(*sig("o_sq", L, t))

                for t in range(NP_T):
                    next_state(2 * t + 1)
                    gate(L, gate_g, 2 * t)
                    next_state(2 * t + 2)
                    gate(L, gate_g, 2 * t + 1)
                    if t:
                        squares(t - 1)
                act.wait_ge(*on("s_now", L, NCH))
                act.dma_start(gla_state_prompt[j, 0].rearrange("h k v -> k h v"),
                              s_now[:, 0, :].rearrange("p (h v) -> p h v", h=GH)).then_inc(*sig("stores_gla", L, n=16))
                act.preload_act_table_set(EXP_LN)
                squares(NP_T - 1)
                act.wait_ge(*on("o_sq", L, NP_T - 1))
                rstd_guess(ost[:, 0, 0:16], ost[:, 2, 0:16], ost[:, 3, 0:16], 1.0 / GDV, (L, "o", 0))
                for b in range(DB):
                    act.wait_ge(*on("s_new", L, b))
                    for h in range(GH):
                        copy(s_in[:, b % 3, h, :], s_in[:, b % 3, h, :], fac[:, h, NCH + b:NCH + b + 1])\
                            .then_inc(*sig("s_end", L, b))
                    act.wait_ge(*on("s_end", L, b))
                    act.dma_start(gla_state_sample[j, b].rearrange("h k v -> k h v"), s_in[:, b % 3])\
                        .then_inc(*sig(f"s_stored{b % 3}", L, b, n=16))
                squares(SMP)
                act.wait_ge(*on("o_sq", L, SMP))
                rstd_guess(ost[0:NS, 0, 16:20], ost[0:NS, 2, 16:20], ost[0:NS, 3, 16:20], 1.0 / GDV, (L, "o", 1))
                for t in range(TILES):
                    for half in range(2):
                        out_hi(L, t, half)

            def dsa(L):
                norm(L)
                for s in range(3):
                    act.wait_ge(*on(f"s_stored{s}", L - 1, max(b for b in range(DB) if b % 3 == s)))
                act.wait_ge(*on("stores_gla", L - 1))
                f_out((L, "ikw"), ik[:], "ik")
                for y in range(2):
                    for part, c in PARTS:
                        act.wait_ge(*on("proj", (L, "iq", y), part))
                        for h in range(2):
                            copy(iq[:, 2 * y + h, c], psum[h * ID:(h + 1) * ID, bank_of("proj", (L, "iq", y), part), 0:HC])\
                                .then_inc(*sig("iq", (L, "iq", y), part))
                act.wait_ge(*on("ikwT", L, 0))
                copy(ikw[:, 0:NP_T, :], psum[:, bank_of("ikwT", L, 0), :].rearrange("p (t n) -> p t n", t=NP_T)
                     [:, :, 0:ID + IH]).then_inc(*sig("ikw", L, 0))
                act.wait_ge(*on("ikwT", L, 1))
                copy(ikw[0:NS, SMP, :], psum[0:NS, bank_of("ikwT", L, 1), 0:ID + IH]).then_inc(*sig("ikw", L, 1))
                act.wait_ge(*on("ikw", L, 1))
                act.dma_start(idxk_rows_prompt[0, 0].rearrange("(t p) d -> p t d", p=P), ikw[:, 0:NP_T, 0:ID])\
                    .then_inc(*sig("stores_ik", 0, n=16))
                act.dma_start(idxk_rows_sample[0].rearrange("b q d -> (b q) d"), ikw[0:NS, SMP, 0:ID])\
                    .then_inc(*sig("stores_ik", 1, n=16))
                sc = ID ** -0.5 * IH ** -0.5
                n = 0
                for t in range(1, NP_T):
                    for h in range(IH):
                        act.wait_ge(*on("idx", L, t, h))
                        if n >= 2:
                            act.wait_ge(*on("relu_used", L, n - 2))
                        act.activation(relu_p[:, n % 2, 0:(t + 1) * P], psum[:, bank_of("idx", L, t, h), 0:(t + 1) * P],
                                       ACT.Relu, scale=sc).then_inc(*sig("idx_relu", L, t, h))
                        n += 1
                for c in range(2):
                    for b in range(DB):
                        act.wait_ge(*on("pages_used", L, c, b))
                        if (c, b) >= (0, 2):
                            q = c * DB + b - 2
                            act.wait_ge(*on("idx_s", L, q // DB, q % DB))
                        copy(ik_old[:, b % 2, :], psum[0:ID, bank_of("oldT", L, c, b), :])\
                            .then_inc(*sig("ik_old", L, c, b))
                    act.wait_ge(*on("idx_s", L, c))
                    act.activation(relu_s[:, c * BLK:(c + 1) * BLK], psum[:, c, :], ACT.Relu, scale=sc)\
                        .then_inc(*sig("idx_relu_s", L, c))
                act.wait_ge(*on("idx_s", L, 2))
                act.activation(relu_s[:, PAST:KEYS], psum[:, 2, 0:NS], ACT.Relu, scale=sc)\
                    .then_inc(*sig("idx_relu_s", L, 2))

                def k_rows(n):
                    for t in range(TILES):
                        if n:
                            act.wait_ge(*on("dkT", L, 0, t))
                            act.wait_ge(*on(f"stores_k{t}", 0))
                        t_out((L, "k", n), t, k_st[0:rows(t), t, :], "k_st")
                        act.wait_ge(*on("k_st", (L, "k", n), t))
                        dst = k_rows_prompt[0, 0, t * P:(t + 1) * P] if t < NP_T \
                            else k_rows_sample[0].rearrange("b q h e -> (b q) h e")
                        act.dma_start(dst.rearrange("t h e -> t (h e)")[:, n * BLK:(n + 1) * BLK],
                                      k_st[0:rows(t), t, :]).then_inc(*sig(f"stores_k{t}", n, n=16))

                def k_turned(n):
                    for t in range(TILES):
                        act.wait_ge(*on("dkT", L, n, t))
                        src = psum[:, bank_of("dkT", L, n, t), :].rearrange("p (h t) -> p h t", h=4)[:, :, 0:rows(t)]
                        dst = k_d[:, 4 * n:4 * n + 4, cols(t)] if t < NP_T else ks_d[:, 4 * n:4 * n + 4, :]
                        copy(dst, src).then_inc(*sig("k_d", L, n, t))

                def q_out(x):
                    for h in (2 * x, 2 * x + 1):
                        f_out((L, "q", h), q_d[:, h, :], "q_d", sample=qs_d[:, h, :])

                k_rows(0)
                q_out(0)
                k_turned(0)
                k_rows(1)
                q_out(1)
                k_turned(1)
                q_out(2)
                q_out(3)
                act.wait_ge(*on("score_s", L, 2))
                for n in range(2):
                    for t in range(TILES):
                        t_out((L, "v", n), t, v_d[0:rows(t), t, n * BLK:(n + 1) * BLK], "v_d")
                        if n:
                            act.wait_ge(*on("v_d", (L, "v", n), t))
                            dst = v_rows_prompt[0, 0, t * P:(t + 1) * P] if t < NP_T \
                                else v_rows_sample[0].rearrange("b q h e -> (b q) h e")
                            act.dma_start(dst.rearrange("t h e -> t (h e)"), v_d[0:rows(t), t, :])\
                                .then_inc(*sig("stores_v", t, n=16))
                for k in range(KT):
                    gate(L, gate_d, k)
                act.preload_act_table_set(EXP_LN)

                units = [(t, h) for t in range(NP_T) for h in range(DH)]
                for t in range(TILES):
                    act.wait_ge(*on(f"stores_k{t}", 1))

                def pt_out(n):
                    t, h = units[n]
                    act.wait_ge(*on("PT", L, n))
                    if n >= 2:
                        act.wait_ge(*on("O", L, n - 2))
                    copy(pt_at[:, n % 2, 0:(t + 1) * P], psum[:, bank_of("PT", L, n), 0:(t + 1) * P])\
                        .then_inc(*sig("PT_read", L, n))

                def branch_hi(m):
                    t, h = units[4 * m]
                    act.wait_ge(*on("oT_read", L, t, h // 4))
                    copy(h_hi[:, h:h + 4, cols(t)], tmp_d[:].rearrange("p (k t) -> p k t", k=4))\
                        .then_inc(*sig("h_hi", (L, "out"), t, h // 4))

                for n in range(len(units) + 3):
                    if n < len(units):
                        t, h = units[n]
                        act.wait_ge(*on("s_shift", L, n))
                        if n >= 2:
                            act.wait_ge(*on("PT", L, n - 2))
                        act.activation(p_at[:, n % 2, 0:(t + 1) * P], s_at[:, n % 2, 0:(t + 1) * P], ACT.Exp,
                                       bias=ast[:, n % 2, 1:2], scale=HD ** -0.5,
                                       accum_out=ast[:, n % 2, 2:3]).then_inc(*sig("p_exp", L, n))
                    if 1 <= n <= len(units):
                        pt_out(n - 1)
                    if n >= 3 and (n - 3) % 4 == 3:
                        branch_hi((n - 3) // 4)

                for grp in range(2):
                    for bl in range(4):
                        b = 4 * grp + bl
                        for pg in range(NPAGE):
                            act.wait_ge(*on("pages_used", L, "kT", b, pg, 0))
                            q = b * NPAGE + pg
                            if q >= 2:
                                act.wait_ge(*on("SS_page", L, (q - 2) // NPAGE, (q - 2) % NPAGE))
                            copy(kt_s[:, q % 2, 0:4, :],
                                 psum[:, bank_of("KT", L, b, pg, 0), :].rearrange("p (h t) -> p h t", h=4))\
                                .then_inc(*sig("kt_s0", L, b, pg))
                    act.wait_ge(*on("ss_shift", L, grp))
                    if grp:
                        act.wait_ge(*on("PsT", L, 0, 2))
                    act.activation(p_s[:], wide[:, 0:KEYS], ACT.Exp, bias=ast[:, 0, 1:2], scale=HD ** -0.5,
                                   accum_out=ast[:, 0, 2:3]).then_inc(*sig("ss_read", L, grp))
                    for x in range(3):
                        act.wait_ge(*on("PsT", L, grp, x))
                        if grp:
                            act.wait_ge(*on("Os", L, 0))
                        b = bank_of("PsT", L, grp, x)
                        if x < 2:
                            copy(pt_s[:, 4 * x:4 * x + 4, :], psum[:, b, :].rearrange("p (g r) -> p g r", g=4))\
                                .then_inc(*sig("pt_s", L, grp, x))
                        else:
                            copy(ptn_s[:], psum[0:NS, b, 0:P]).then_inc(*sig("pt_s", L, grp, x))
                act.wait_ge(*on("os_read", L))
                copy(h_hi[:, :, SEQ:TOK], tmp_d2[:].rearrange("p (h t) -> p h t", h=DH))\
                    .then_inc(*sig("h_hi", (L, "out"), SMP, 1))

            def pooling(L):
                norm(L)
                act.wait_ge(*on("stores_v", "all"))
                act.wait_ge(*on("stores_ik", "all"))
                for k in range(KT):
                    f_out((L, "u", k), u_p[:, k, PADW:], "u", sample=u_new[:, k, :])
                act.wait_ge(*on("u", (L, "u", KT - 1), 1))
                copy(u_s[:, :, :, PADW:], u_new[:].rearrange("p k (b q) -> p k b q", b=DB)).then_inc(*sig("u_placed", L))
                for half in range(2):
                    act.wait_ge(*on("oldP", L, half))
                    src = psum[:, bank_of("oldP", L, half), :].rearrange("p (k r) -> p k r", k=4)
                    for k in range(4):
                        copy(u_s[:, 4 * half + k, :, 1:PADW],
                             src[:, k, 0:DB * STATE].rearrange("p (b r) -> p b r", b=DB))\
                            .then_inc(*sig("u_old", L, half))
                for k in range(KT):
                    gate(L, gate_p, k)
                act.preload_act_table_set(EXP_LN)
                for part, m in ((0, STATE), (1, NS)):
                    for half in range(2):
                        act.wait_ge(*on("rowsT", L, part, half))
                        copy(new_rows[0:m, part, half * BLK:(half + 1) * BLK],
                             psum[0:m, bank_of("rowsT", L, part, half), :]).then_inc(*sig("pool_rows", L, part, half))
                act.wait_ge(*on("pool_rows", L, 1, 1))
                act.dma_start(pool_state_prompt[0, 0], new_rows[0:STATE, 0, :]).then_inc(*sig("stores_pool", 0, n=16))
                for b in range(DB):
                    act.dma_start(pool_state_sample[0, b, STATE - DQ:, :], new_rows[b * DQ:(b + 1) * DQ, 1, :])\
                        .then_inc(*sig("stores_pool", 1, b, n=16))
                act.dma_start(pool_state_sample[0, :, 0:STATE - DQ, :], state_pool[0, :, DQ:, :])\
                    .then_inc(*sig("stores_pool", 2, n=16))
                for k in range(KT):
                    act.wait_ge(*on("d_tmp", L, k))
                    copy(d_hi[:, k, :], d_tmp[:]).then_inc(*sig("d_hi", L, k))
                for k in range(KT):
                    act.wait_ge(*on("y_read", (L, "y", k), 1))
                    copy(h_hi[:, k, :], d_tmp[:]).then_inc(*sig("y_hi", L, k))

            act.preload_act_table_set(EXP_LN)
            act.wait_ge(*on("const", "first"))
            for L, kind in enumerate(KINDS):
                (gla, dsa, pooling)[kind](L)
            norm(len(KINDS), last=True)

        @block.vector
        def _(dve):
            def link(ins, name="vec_chain"):
                ins.then_inc(*sig(name, count.get(name, 0)))
                dve.wait_ge(semaphore(name), count[name])

            def refine(m, sq, y, a, b, out, n_inv, key, last_key):
                link(dve.tensor_scalar(m, sq, n_inv, RMS_EPS, ALU.mult, ALU.add))
                dve.wait_ge(*on("rstd_y", *key))
                link(dve.tensor_tensor(a, y, m, ALU.mult))
                link(dve.tensor_tensor(a, a, y, ALU.mult))
                link(dve.tensor_scalar(b, a, -0.5, 1.5, ALU.mult, ALU.add))
                link(dve.tensor_tensor(out, y, b, ALU.mult))

            def norm_lo(L, t):
                r = rows(t)
                for half in range(2):
                    dve.wait_ge(*on("h_hi", L, t, half))
                    b = bank_of("nT", L, t, half)
                    k = slice(4 * half, 4 * half + 4)
                    dve.tensor_tensor(h_lo[:, k, cols(t)],
                                      psum[:, b, :].rearrange("p (k t) -> p k t", k=4)[:, :, 0:r],
                                      h_hi[:, k, cols(t)].bitcast(F32), ALU.subtract)\
                        .then_inc(*sig("h_lo", L, t, half))

            def norm(L, last=False):
                dve.wait_ge(*on("gain", L))
                for t in range(TILES):
                    r = rows(t)
                    s = st[0:r, t % 2, :]
                    dve.wait_ge(*on("sumsq", L, t))
                    refine(s[:, 1:2], s[:, 0:1], s[:, 3:4], s[:, 4:5], s[:, 5:6], s[:, 6:7], 1.0 / D, (L, t), None)
                    if t >= 2:
                        if last:
                            dve.wait_ge(*on(f"stores_y{t % 2}", t - 2))
                        else:
                            dve.wait_ge(*on("nT", L, t - 2, 1))
                    dve.scalar_tensor_tensor(out=xn[0:r, t % 2, :], in0=X[0:r, t, :], scalar=s[:, 6:7],
                                             in1=gain[0:r, :], op0=ALU.mult, op1=ALU.mult).then_inc(*sig("xn", L, t))
                    if t and not last:
                        norm_lo(L, t - 1)
                if not last:
                    norm_lo(L, SMP)

            def resid(L):
                for n in range(2):
                    for t in range(TILES):
                        r = rows(t)
                        name = (L, "out", n)
                        dve.wait_ge(*on("proj", (name, t)))
                        x = X[0:r, t, n * BLK:(n + 1) * BLK]
                        dve.tensor_tensor(x, psum[0:r, bank_of("proj", name, t), :], x, ALU.add)\
                            .then_inc(*sig("resid", name, t))

            def out_gated(L, t, half, gate_buf, tmp):
                n = rows(t)
                dve.tensor_tensor(tmp.rearrange("p (k t) -> p k t", k=4),
                                  psum[:, bank_of("oT", L, t, half), :].rearrange("p (k t) -> p k t", k=4)[:, :, 0:n],
                                  gate_buf[:, 4 * half:4 * half + 4, cols(t)], ALU.mult)\
                    .then_inc(*sig("oT_read", L, t, half))

            def out_lo(L, t, half, tmp):
                k = slice(4 * half, 4 * half + 4)
                dve.wait_ge(*on("h_hi", (L, "out"), t, half))
                dve.tensor_tensor(h_lo[:, k, cols(t)], tmp.rearrange("p (k t) -> p k t", k=4),
                                  h_hi[:, k, cols(t)].bitcast(F32), ALU.subtract)\
                    .then_inc(*sig("h_lo", (L, "out"), t, half))

            def gla(L):
                norm(L)
                dve.wait_ge(*on("const", "all"))
                dve.wait_ge(*on("gla_small", L))
                if L:
                    dve.wait_ge(*on("stores_pool", "all"))
                for h in range(GH):
                    dve.wait_ge(*on("z_abs", L, h))
                    dve.tensor_scalar(qg[:, h, 0:SEQ], psum[:, bank_of("z", L, h), :], b_a[:, h:h + 1], 0.0,
                                      ALU.add, ALU.min).then_inc(*sig("z_read", L, h))
                dve.wait_ge(*on("z_abs", L, "s"))
                for h in range(GH):
                    dve.tensor_scalar(qg[:, h, SEQ:TOK], psum[:, bank_of("z", L, "s"), h * NS:(h + 1) * NS],
                                      b_a[:, h:h + 1], 0.0, ALU.add, ALU.min).then_inc(*sig("z_read", L, "s"))
                dve.wait_ge(*on("z_read", L, "s"))
                dve.wait_ge(*on("z_soft", L))
                link(dve.tensor_tensor(qg[:], qg[:], soft[:], ALU.subtract))
                for h in range(GH):
                    ins = dve.tensor_tensor_scan(kg[:, h, :], no_reset[:], qg[:, h, :], 0.0, ALU.mult, ALU.add)
                    if h < GH - 1:
                        ins.then_inc(*sig("vec_chain", count.get("vec_chain", 0)))
                link(ins)
                kc = kg[:, :, 0:SEQ].rearrange("p h (c t) -> p h c t", c=NCH)
                qc = qg[:, :, 0:SEQ].rearrange("p h (c t) -> p h c t", c=NCH)
                link(dve.tensor_copy(mid[:], kc[:, :, :, CH // 2 - 1]))
                for h in range(GH):
                    dve.tensor_tensor(qc[:, h], kc[:, h], mid[:, h, :].unsqueeze(2).broadcast_to([P, NCH, CH]),
                                      ALU.subtract).then_inc(*sig("decay_h", L, h))
                dve.tensor_copy(qg[:, :, SEQ:TOK], kg[:, :, SEQ:TOK]).then_inc(*sig("decay_h", L, "s"))
                dve.wait_ge(*on("decay_h", L, "s"))
                dve.tensor_tensor(fac[:, :, 0:NCH - 1], qc[:, :, 0:NCH - 1, CH - 1], mid[:, :, 1:NCH], ALU.add)\
                    .then_inc(*sig("fac_part", L, 0))
                dve.tensor_copy(fac[:, :, NCH - 1:NCH], qc[:, :, NCH - 1:NCH, CH - 1])\
                    .then_inc(*sig("fac_part", L, 1))
                dve.tensor_copy(fac[:, :, NCH:], kg[:, :, SEQ:TOK].rearrange("p h (b q) -> p h b q", b=DB)[:, :, :, DQ - 1])\
                    .then_inc(*sig("fac", L, also=()))
                dve.wait_ge(*on("fac", L))
                dve.tensor_copy(mid[:, :, 0:1], mid[:, :, 0:1]).then_inc(*sig("decay", L))
                dve.wait_ge(*on("k_decay", L))
                for h in range(GH):
                    name = (L, "k", h)
                    for part, c in PARTS:
                        dve.wait_ge(*on("proj", name, part))
                        dve.tensor_tensor(kg[:, h, c], psum[:, bank_of("proj", name, part), 0:HC],
                                          kg[:, h, c], ALU.mult).then_inc(*sig("k_gated", name, part))
                dve.wait_ge(*on("q_decay", L))
                for h in range(GH):
                    name = (L, "q", h)
                    for part, c in PARTS:
                        dve.wait_ge(*on("proj", name, part))
                        dve.scalar_tensor_tensor(out=qg[:, h, c],
                                                 in0=psum[:, bank_of("proj", name, part), 0:HC],
                                                 scalar=GDK ** -0.5, in1=qg[:, h, c], op0=ALU.mult,
                                                 op1=ALU.mult).then_inc(*sig("q_gated", name, part))
                dve.wait_ge(*on("q_gated", (L, "q", GH - 1), 1))
                for h in range(GH):
                    dve.tensor_tensor(q_seq[:, h], qg[:, h, SEQ:TOK].unsqueeze(1).broadcast_to([P, DB, NS]),
                                      seq_col[:], ALU.mult).then_inc(*sig("q_seq", L))

                def add_state(c):
                    dve.wait_ge(*on("state", L, c))
                    b = bank_of("state", L, c, 0)
                    src = wide[:, b * 512:b * 512 + GH * GDV]
                    if c == 0:
                        dve.tensor_copy(s_sum[:], src).then_inc(*sig("s_sum", L, c))
                    else:
                        dve.wait_ge(*on("s_now", L, c))
                        dve.tensor_tensor(s_sum[:], src, s_now[:, c % 2, :], ALU.add).then_inc(*sig("s_sum", L, c))

                def out_rows(t):
                    r = rows(t)
                    dve.wait_ge(*on("o", L, t))
                    b = bank_of("o", L, t, 0)
                    dve.tensor_copy(v_g[0:r, t, :], wide[0:r, b * 512:b * 512 + D]).then_inc(*sig("o_out", L, t))

                def normalise(t):
                    r = rows(t)
                    for h in range(GH):
                        x = v_g[0:r, t, h * GDV:(h + 1) * GDV]
                        dve.scalar_tensor_tensor(out=x, in0=x, scalar=ost[0:r, 4, 4 * t + h:4 * t + h + 1],
                                                 in1=g_on[0:r, :], op0=ALU.mult, op1=ALU.mult)\
                            .then_inc(*sig("o_norm", L, t))

                for t in range(NP_T):
                    dve.wait_ge(*on("att", L, t))
                    dve.tensor_tensor(att_g[:], psum[:, 0, :].rearrange("p (h t) -> p h t", h=GH),
                                      chunk_tri[:].unsqueeze(1).broadcast_to([P, GH, P]), ALU.mult)\
                        .then_inc(*sig("att_m", L, t))
                    add_state(2 * t)
                    add_state(2 * t + 1)
                    out_rows(t)
                dve.wait_ge(*on("att", L, SMP))
                dve.tensor_tensor(att_g[0:NS, :, 0:NS], psum[0:NS, 0, 0:GH * NS].rearrange("p (h t) -> p h t", h=GH),
                                  seq_tri[:].unsqueeze(1).broadcast_to([NS, GH, NS]), ALU.mult)\
                    .then_inc(*sig("att_m", L, SMP))

                def k_of(b):
                    if b >= 2:
                        dve.wait_ge(*on("s_state", L, b - 2))
                    dve.tensor_scalar(k_seq[:, b % 2, :], k_tok[0:NS, SMP, :], seq_row[:, b:b + 1], None, ALU.mult)\
                        .then_inc(*sig("k_seq", L, b))

                dve.wait_ge(*on("k_tok", L, SMP))
                k_of(0)
                k_of(1)
                dve.wait_ge(*on("o_sq", L, NP_T - 1))
                c = slice(0, 16)
                refine(ost[:, 1, c], ost[:, 0, c], ost[:, 3, c], ost[:, 1, c], ost[:, 2, c], ost[:, 4, c],
                       1.0 / GDV, (L, "o", 0), None)
                for b in range(DB):
                    dve.wait_ge(*on("s_state", L, b))
                    pb = bank_of("s_state", L, b, 0)
                    dve.tensor_tensor(s_in[:, b % 3].rearrange("p h v -> p (h v)"), wide[:, pb * 512:pb * 512 + D],
                                      s_in[:, b % 3].rearrange("p h v -> p (h v)"), ALU.add)\
                        .then_inc(*sig("s_new", L, b))
                    if b + 2 < DB:
                        k_of(b + 2)
                    if b % 2:
                        normalise(b // 2)
                out_rows(SMP)
                dve.wait_ge(*on("o_sq", L, SMP))
                c = slice(16, 20)
                refine(ost[0:NS, 1, c], ost[0:NS, 0, c], ost[0:NS, 3, c], ost[0:NS, 1, c], ost[0:NS, 2, c],
                       ost[0:NS, 4, c], 1.0 / GDV, (L, "o", 1), None)
                normalise(SMP)
                for t in range(TILES):
                    for half in range(2):
                        dve.wait_ge(*on("oT", L, t, half))
                        if t:
                            dve.wait_ge(*on("h_lo", (L, "out"), t - 1, half))
                        out_gated(L, t, half, gate_g, tmp_og[:, half, 0:4 * rows(t)])
                    for half in range(2):
                        out_lo(L, t, half, tmp_og[:, half, 0:4 * rows(t)])
                resid(L)

            def dsa(L):
                norm(L)
                for s in range(3):
                    dve.wait_ge(*on(f"s_stored{s}", L - 1, max(b for b in range(DB) if b % 3 == s)))
                dve.wait_ge(*on("stores_gla", L - 1))
                dve.wait_ge(*on("iq", (L, "iq", 1), 1))
                for h in range(IH):
                    dve.tensor_tensor(iq_seq[:, h], iq[:, h, SEQ:TOK].unsqueeze(1).broadcast_to([ID, DB, NS]),
                                      seq_col[0:ID], ALU.mult).then_inc(*sig("iq_seq", L))
                dve.wait_ge(*on("ikw", L, 1))
                for h in range(IH):
                    link(dve.tensor_copy(w_stack[h * NS:(h + 1) * NS, :], ikw[0:NS, SMP, ID + h:ID + h + 1]))
                dve.tensor_scalar(w_sel[:], stack4[:], w_stack[:], None, ALU.mult).then_inc(*sig("w_sel", L))
                n = 0
                for t in range(1, NP_T):
                    w = (t + 1) * P
                    for h in range(IH):
                        dve.wait_ge(*on("idx_relu", L, t, h))
                        s = ikw[:, t, ID + h:ID + h + 1]
                        if h == 0:
                            ins = dve.tensor_scalar(bias_p[t][:], relu_p[:, n % 2, 0:w], s, None, ALU.mult)
                        else:
                            ins = dve.scalar_tensor_tensor(out=bias_p[t][:], in0=relu_p[:, n % 2, 0:w], scalar=s,
                                                           in1=bias_p[t][:], op0=ALU.mult, op1=ALU.add)
                        ins.then_inc(*sig("relu_used", L, n))
                        dve.wait_ge(*on("relu_used", L, n))
                        n += 1
                    diag = bias_p[t][:, t * P:(t + 1) * P]
                    link(dve.tensor_tensor(diag, diag, future_p[:], ALU.add))
                for c, w in enumerate((BLK, BLK, NS)):
                    dve.wait_ge(*on("score_mm", L, c))
                    src = psum[0:NS, bank_of("score_s", L, c), 0:w]
                    dst = score_s[:, c * BLK:c * BLK + w]
                    if c < 2:
                        dve.tensor_copy(dst, src).then_inc(*sig("score_s", L, c))
                    else:
                        dve.tensor_tensor(dst, src, future_s[:], ALU.add).then_inc(*sig("score_s", L, c))
                dve.wait_ge(*on("score_s", L, 2))

                def top(scores, m, k):
                    for _ in range(k // 8):
                        link(dve.max(out=top8[0:m, :], in_=scores))
                        link(dve.match_replace(out=scores, in_to_replace=top8[0:m, :], in_values=scores,
                                               imm_value=TAKEN))

                for t in range(1, NP_T):
                    top(bias_p[t][:], P, TOPK_P)
                    link(dve.tensor_scalar(bias_p[t][:], bias_p[t][:], TAKEN, FUTURE, ALU.not_equal, ALU.mult))
                top(score_s[:], NS, TOPK_S)
                dve.tensor_scalar(bias_s[:], score_s[:], TAKEN, FUTURE, ALU.not_equal, ALU.mult)\
                    .then_inc(*sig("bias_s", L))

                units = [(t, h) for t in range(NP_T) for h in range(DH)]
                for t in range(TILES):
                    dve.wait_ge(*on(f"stores_k{t}", 1))
                dve.wait_ge(*on("dkT", L, 1, SMP))

                def shift(n):
                    t, h = units[n]
                    w = (t + 1) * P
                    dve.wait_ge(*on("S", L, n))
                    if n >= 2:
                        dve.wait_ge(*on("p_exp", L, n - 2))
                    dve.tensor_tensor_reduce(out=s_at[:, n % 2, 0:w], in0=psum[:, bank_of("S", L, n), 0:w],
                                             in1=(bias_p[t][:] if t else future_p[:]), scale=1.0, scalar=TAKEN,
                                             op0=ALU.add, op1=ALU.max, accum_out=ast[:, n % 2, 0:1])\
                        .then_inc(*sig("S_read", L, n))
                    dve.wait_ge(*on("S_read", L, n))
                    dve.tensor_scalar(ast[:, n % 2, 1:2], ast[:, n % 2, 0:1], -HD ** -0.5, None, ALU.mult)\
                        .then_inc(*sig("s_shift", L, n))

                def normalise(n):
                    t, h = units[n]
                    dve.wait_ge(*on("p_exp", L, n))
                    link(dve.reciprocal(ast[:, n % 2, 3:4], ast[:, n % 2, 2:3]))
                    x = p_at[:, n % 2, 0:(t + 1) * P]
                    dve.tensor_scalar(x, x, ast[:, n % 2, 3:4], None, ALU.mult).then_inc(*sig("p_norm", L, n))

                def branch(m):
                    t, h = units[4 * m]
                    dve.wait_ge(*on("O", L, 4 * m + 3))
                    if m:
                        pt, ph = units[4 * m - 4]
                        dve.wait_ge(*on("h_lo", (L, "out"), pt, ph // 4))
                    dve.tensor_tensor(tmp_d[:].rearrange("p (k t) -> p k t", k=4),
                                      psum[:, (4, 5)[m % 2], :].rearrange("p (k t) -> p k t", k=4),
                                      gate_d[:, h:h + 4, cols(t)], ALU.mult).then_inc(*sig("oT_read", L, t, h // 4))
                    out_lo(L, t, h // 4, tmp_d[:])

                for n in range(len(units) + 3):
                    if n < len(units):
                        shift(n)
                    if 1 <= n <= len(units):
                        normalise(n - 1)
                    if n >= 3 and (n - 3) % 4 == 3:
                        branch((n - 3) // 4)

                dve.wait_ge(*on("S", L, len(units) - 1))
                link(dve.memset(q_heads[:], 0.0))
                for h in range(DH):
                    dve.tensor_copy(q_heads[:, h, :, h * DQ:(h + 1) * DQ],
                                    qs_d[:, h, :].rearrange("p (b q) -> p b q", b=DB)).then_inc(*sig("q_heads", L))
                for grp in range(2):
                    for bl in range(4):
                        b = 4 * grp + bl
                        for pg in range(NPAGE):
                            dve.wait_ge(*on("pages_used", L, "kT", b, pg, 1))
                            q = b * NPAGE + pg
                            if q >= 2:
                                dve.wait_ge(*on("SS_page", L, (q - 2) // NPAGE, (q - 2) % NPAGE))
                            dve.tensor_copy(kt_s[:, q % 2, 4:8, :],
                                            psum[:, bank_of("KT", L, b, pg, 1), :].rearrange("p (h t) -> p h t", h=4))\
                                .then_inc(*sig("kt_s1", L, b, pg))
                    dve.wait_ge(*on("SS", L, grp))
                    link(dve.tensor_reduce(ast[:, 0, 0:1], wide[:, 0:KEYS], AX.X, ALU.max))
                    dve.tensor_scalar(ast[:, 0, 1:2], ast[:, 0, 0:1], -HD ** -0.5, None, ALU.mult)\
                        .then_inc(*sig("ss_shift", L, grp))
                    dve.wait_ge(*on("ss_read", L, grp))
                    link(dve.reciprocal(ast[:, 0, 3:4], ast[:, 0, 2:3]))
                    dve.tensor_scalar(p_s[:], p_s[:], ast[:, 0, 3:4], None, ALU.mult).then_inc(*sig("ps_norm", L, grp))
                dve.wait_ge(*on("Os", L, 1))
                dve.tensor_tensor(tmp_d2[:].rearrange("p (h t) -> p h t", h=DH),
                                  psum[:, 3, 0:DH * NS].rearrange("p (h t) -> p h t", h=DH),
                                  gate_d[:, :, SEQ:TOK], ALU.mult).then_inc(*sig("os_read", L))
                dve.wait_ge(*on("h_hi", (L, "out"), SMP, 1))
                dve.tensor_tensor(h_lo[:, :, SEQ:TOK], tmp_d2[:].rearrange("p (h t) -> p h t", h=DH),
                                  h_hi[:, :, SEQ:TOK].bitcast(F32), ALU.subtract)\
                    .then_inc(*sig("h_lo", (L, "out"), SMP, 1))
                resid(L)

            def pooling(L):
                norm(L)
                dve.wait_ge(*on("stores_v", "all"))
                dve.memset(u_p[:, :, 0:PADW], 0.0).then_inc(*sig("u_pad", L))
                dve.wait_ge(*on("u_pad", L))
                link(dve.reciprocal(inv_cnt[:], inv_cnt[:]))
                dve.wait_ge(*on("pool_small"))
                dve.wait_ge(*on("u_old", L, 1))
                for k in range(KT):
                    grp = k // 2
                    w = WINDOWS[grp]
                    src, src_s = u_p[:, k, :], u_s[:, k]
                    for i in range(grp + 1):
                        s = 1 << i
                        dst, dst_s = win[:, i % 2, :], win_s[:, i % 2]
                        dve.tensor_tensor(dst[:, 2 * s - 1:], src[:, 2 * s - 1:], src[:, s - 1:PADW + SEQ - s],
                                          ALU.add).then_inc(*sig("vec_chain", count.get("vec_chain", 0)))
                        link(dve.tensor_tensor(dst_s[:, :, 2 * s:], src_s[:, :, 2 * s:],
                                               src_s[:, :, s:PADW + DQ - s], ALU.add))
                        src, src_s = dst, dst_s
                    if k:
                        dve.wait_ge(*on("d_lo", L, k - 1))
                    dve.scalar_tensor_tensor(out=d_tmp[:, 0:SEQ], in0=src[:, PADW:], scalar=1.0 / w,
                                             in1=u_p[:, k, PADW:], op0=ALU.mult, op1=ALU.subtract)\
                        .then_inc(*sig("vec_chain", count.get("vec_chain", 0)))
                    dve.tensor_tensor(small_d[:, 0:w - 1], src[:, PADW:PADW + w - 1], inv_cnt[:, 0:w - 1], ALU.mult)\
                        .then_inc(*sig("vec_chain", count.get("vec_chain", 0)))
                    link(dve.scalar_tensor_tensor(out=d_tmp[:, SEQ:TOK].rearrange("p (b q) -> p b q", b=DB),
                                                  in0=src_s[:, :, PADW:], scalar=1.0 / w, in1=u_s[:, k, :, PADW:],
                                                  op0=ALU.mult, op1=ALU.subtract))
                    dve.tensor_tensor(d_tmp[:, 0:w - 1], small_d[:, 0:w - 1], u_p[:, k, PADW:PADW + w - 1],
                                      ALU.subtract).then_inc(*sig("d_tmp", L, k))
                    dve.wait_ge(*on("d_hi", L, k))
                    dve.tensor_tensor(d_lo[:, k, :], d_tmp[:], d_hi[:, k, :].bitcast(F32), ALU.subtract)\
                        .then_inc(*sig("d_lo", L, k))
                dve.wait_ge(*on("gate", (L, "g", KT - 1), 1))
                dve.wait_ge(*on("d_lo", L, KT - 1))
                for k in range(KT):
                    name = (L, "y", k)
                    if k:
                        dve.wait_ge(*on("h_lo", L, "y", k - 1))
                    for part, c in PARTS:
                        dve.wait_ge(*on("proj", name, part))
                        dve.scalar_tensor_tensor(out=d_tmp[:, c],
                                                 in0=psum[:, bank_of("proj", name, part), 0:HC],
                                                 scalar=scale_p[:, k:k + 1], in1=gate_p[:, k, c], op0=ALU.mult,
                                                 op1=ALU.mult).then_inc(*sig("y_read", name, part))
                    dve.wait_ge(*on("y_hi", L, k))
                    dve.tensor_tensor(h_lo[:, k, :], d_tmp[:], h_hi[:, k, :].bitcast(F32), ALU.subtract)\
                        .then_inc(*sig("h_lo", L, "y", k,
                                       also=[((L, "out"), t, 1) for t in range(TILES)] if k == KT - 1 else ()))
                resid(L)

            dve.wait_ge(*on("const", "first"))
            for L, kind in enumerate(KINDS):
                (gla, dsa, pooling)[kind](L)
            norm(len(KINDS), last=True)


_INS = ["x_prompt", "x_sample", "state_gla", "cache_k", "cache_v", "cache_idx_k", "state_pool", "page_table",
        "gla_norm", "gla_w_in", "gla_w_a2", "gla_b_a", "gla_out_norm", "gla_w_out", "dsa_norm", "dsa_w_in",
        "dsa_w_out", "pool_norm", "pool_w_in", "pool_w_grp", "pool_scale", "pool_w_out", "final_norm"]
_OUTS = [(1, SEQ, D), (DB, DQ, D), (2, 1, GH, GDK, GDV), (2, DB, GH, GDK, GDV), (1, 1, SEQ, DH, HD),
         (1, DB, DQ, DH, HD), (1, 1, SEQ, DH, HD), (1, DB, DQ, DH, HD), (1, 1, SEQ, ID), (1, DB, DQ, ID),
         (1, 1, STATE, D), (1, DB, STATE, D)]


def kernel(**inputs):
    import numpy as _np
    import concourse.bacc as _bacc
    from concourse import mybir as _mybir
    from concourse.bass_utils import run_bass_kernel_spmd as _run

    arrays = {f"in_{name}_dram": _np.ascontiguousarray(inputs[name]) for name in _INS}
    plan = Plan()
    for _ in range(2):
        nc = _bacc.Bacc("TRN2", target_bir_lowering=False, num_devices=1, dynamic_dma_scratch_size=1024)
        args = [nc.dram_tensor(n, a.shape, _mybir.dt.from_np(a.dtype), kind="ExternalInput").ap()
                for n, a in arrays.items()]
        outs = [nc.dram_tensor(f"out_{i}_dram", shape, _mybir.dt.float32, kind="ExternalOutput").ap()
                for i, shape in enumerate(_OUTS)]
        program(nc, plan, *args, outs)
    r = _run(nc, [arrays], core_ids=[0])
    return tuple(r.results[0][f"out_{i}_dram"] for i in range(len(_OUTS)))
```

```python
from contextlib import ExitStack

import concourse.bass as bass
from concourse import mybir

F32 = mybir.dt.float32
F32R = mybir.dt.float32r
BF16 = mybir.dt.bfloat16
I32 = mybir.dt.int32
ALU = mybir.AluOpType
ACT = mybir.ActivationFunctionType
AX = mybir.AxisListType

P = 128
D = 1024
KT = D // P
SEQ, DB, DQ = 512, 8, 4
NS = DB * DQ
NP_T = SEQ // P
TILES = NP_T + 1
SMP = NP_T
TOK = SEQ + NS
HC = TOK // 2
PARTS = ((0, slice(0, HC)), (1, slice(HC, TOK)))
BLK = 512
HALF = 256
PAST, PAGE = 1024, 128
NPAGE = PAST // PAGE
RMS_EPS = 1e-6
GH, GDK, GDV = 4, 128, 256
CH = 64
NCH = SEQ // CH
TAU = 16.0
RANK = 16
DH, HD = 8, 128
IH, ID = 4, 64
TOPK_P, TOPK_S = 128, 256
KEYS = PAST + NS
WINDOWS = (2, 4, 8, 16)
STATE = 15
PADW = 16
FUTURE = -1e30
TAKEN = -3e38
NBANK = 8
RAW, SPARE = 3, 4
EXP_LN = "natural_log_exp_and_others"
KINDS = (0, 1, 2, 0)


def rows(t):
    return NS if t == SMP else P


def cols(t):
    return slice(t * P, t * P + rows(t))


class Plan:

    def __init__(self):
        self.value, self.bank = {}, {}


def program(nc, plan, x_prompt, x_sample, state_gla, cache_k, cache_v, cache_idx_k, state_pool, page_table,
            gla_norm, gla_w_in, gla_w_a2, gla_b_a, gla_out_norm, gla_w_out, dsa_norm, dsa_w_in, dsa_w_out,
            pool_norm, pool_w_in, pool_w_grp, pool_scale, pool_w_out, final_norm, outs):
    (y_prompt, y_sample, gla_state_prompt, gla_state_sample, k_rows_prompt, k_rows_sample, v_rows_prompt,
     v_rows_sample, idxk_rows_prompt, idxk_rows_sample, pool_state_prompt, pool_state_sample) = outs

    with ExitStack() as ctx:
        sems, count = {}, {}

        def semaphore(name):
            if name not in sems:
                sems[name] = ctx.enter_context(nc.semaphore(name))
            return sems[name]

        def sig(name, *key, also=(), n=1):
            s = semaphore(name)
            count[name] = count.get(name, 0) + n
            for k in (key, ("all",)) + tuple(also):
                plan.value[(name,) + k] = count[name]
            return s, n

        def on(name, *key):
            return semaphore(name), plan.value.get((name,) + key, 1)

        def bank_of(*key):
            return plan.bank.get(key, 0)

        place = {"at": (nc.sbuf_base + 63) // 64 * 64}

        def at(name, shape, dt, offset):
            return nc.alloc_sbuf_tensor_at(name, shape, dt, offset=offset)

        def size(shape, dt):
            n = 2 if dt == BF16 else 4
            for s in shape[1:]:
                n *= s
            return (n + 63) // 64 * 64

        def sb(name, shape, dt=F32):
            o = place["at"]
            place["at"] += size(shape, dt)
            return at(name, shape, dt, o)

        class Region:

            def __init__(self, start, end):
                self.o, self.end = start, end

            def __call__(self, name, shape, dt=F32):
                o = self.o
                self.o += size(shape, dt)
                assert self.o <= self.end, (name, self.o - self.end)
                return at(name, shape, dt, o)

        X = sb("X", [P, TILES, D])
        h_hi = sb("h_hi", [P, KT, TOK], F32R)
        h_lo = sb("h_lo", [P, KT, TOK], F32R)
        raw = sb("raw", [P, RAW, 2048])
        w_hi = sb("w_hi", [P, 2, 2048], F32R)
        w_lo = sb("w_lo", [P, 2, 2048], F32R)
        spare = at("spare", [P, SPARE, 2048], F32, place["at"] - 2 * size([P, 2, 2048], F32))
        ident = sb("ident", [P, P])
        chunk_tri = sb("chunk_tri", [P, P])
        seq_tri = sb("seq_tri", [NS, NS])
        future_p = sb("future_p", [P, P])
        future_s = sb("future_s", [NS, NS])
        stack4 = sb("stack4", [P, NS])
        pick_tok = sb("pick_tok", [NS, DB, NS], BF16)
        seq_col = sb("seq_col", [P, DB, NS], BF16)
        seq_row = sb("seq_row", [NS, DB])
        no_reset = sb("no_reset", [P, TOK], BF16)
        inv_cnt = sb("inv_cnt", [P, PADW])
        cnt_i = sb("cnt_i", [P, PADW])
        b_a = sb("b_a", [P, GH])
        g_on = sb("g_on", [P, GDV])
        w_a2 = sb("w_a2", [RANK, GH * GDK])
        scale_p = sb("scale_p", [P, KT])
        eps = sb("eps", [P, 1])
        one = sb("one", [P, 1])
        ptab = sb("ptab", [1, DB * NPAGE], I32)
        st = sb("st", [P, 2, 8])
        ost = sb("ost", [P, 5, 20])
        sq_junk = sb("sq_junk", [P, D], BF16)
        gain_at = place["at"]
        gain = sb("gain", [P, D])
        xn_at = place["at"]
        xn = sb("xn", [P, 2, D])
        place["at"] += 128
        xn_end = place["at"]
        arena, arena_end = place["at"], nc.sbuf_usable_end

        g = Region(arena, arena_end)
        qg = g("gla_q", [P, GH, TOK])
        kg = g("gla_k", [P, GH, TOK])
        ktok_at = g.o
        k_tok = g("gla_k_tok", [P, TILES, GH * GDK])
        soft = at("gla_soft", [P, GH, TOK], F32, ktok_at)
        gate_g = g("gla_gate", [P, KT, TOK])
        v_g = g("gla_v", [P, TILES, D])
        s_now = g("gla_s_now", [P, 2, GH * GDV])
        s_in = g("gla_s_in", [P, 3, GH, GDV])
        att_g = g("gla_att", [P, GH, P])
        a_t = at("gla_a", [RANK, TOK], F32, g.o)
        q_seq = g("gla_q_seq", [P, GH, DB, NS])
        mid = g("gla_mid", [P, GH, NCH])
        fac = g("gla_fac", [P, GH, 2 * NCH])
        gx = Region(xn_at, xn_end)
        s_sum = gx("gla_s_sum", [P, GH * GDV])
        k_seq = gx("gla_k_seq", [NS, 2, GH * GDK])
        tmp_og = at("tmp_og", [P, 2, BLK], F32, gain_at)

        d = Region(arena, arena_end)
        qk_at = d.o
        q_d = d("dsa_q", [P, DH, SEQ])
        k_d = d("dsa_k", [P, DH, SEQ])
        qk_end = d.o
        idx_pages = at("idx_pages", [P, DB * NPAGE, ID], F32, qk_at)
        v_at = d.o
        v_d = d("dsa_v", [P, TILES, D])
        gate_d = d("dsa_gate", [P, KT, TOK])
        v_end = d.o
        bias_p = [None] + [d(f"dsa_bias{t}", [P, P * (t + 1)]) for t in range(1, NP_T)]
        bias_s = d("dsa_bias_s", [NS, KEYS], BF16)
        ikw = d("dsa_ikw", [P, TILES, ID + IH])
        qs_d = d("dsa_q_s", [P, DH, NS])
        ks_d = d("dsa_k_s", [P, DH, NS])
        ast = d("dsa_ast", [P, 2, 4])
        w_stack = d("dsa_w_stack", [P, 1])
        w_sel = d("dsa_w_sel", [P, NS])
        top8 = d("dsa_top8", [P, 8])
        kst_at = d.o
        k_st = d("dsa_k_st", [P, TILES, BLK])
        kst_end = d.o
        dx = Region(xn_at, xn_end)
        score_s = dx("dsa_score_s", [NS, KEYS])
        tmp_d = dx("dsa_tmp", [P, BLK])
        tmp_d2 = dx("dsa_tmp2", [P, 8 * NS])
        i = Region(v_at, v_end)
        iq = i("idx_q", [ID, IH, TOK])
        iq_seq = i("idx_q_seq", [ID, IH, DB, NS])
        ik = i("idx_k", [ID + IH, TOK])
        ik_old = i("idx_k_old", [ID, 2, BLK])
        relu_p = i("idx_relu", [P, 2, BLK])
        relu_s = i("idx_relu_s", [P, KEYS])
        a = Region(kst_at, kst_end)
        s_at = a("att_s", [P, 2, BLK])
        p_at = a("att_p", [P, 3, BLK])
        pt_at = at("att_pt", [P, 2, BLK], F32, gain_at)
        o = Region(qk_at, qk_end)
        kt_s = o("smp_kt", [P, 2, DH, PAGE])
        q_heads = o("smp_q", [P, DH, DB, NS])
        p_s = o("smp_p", [P, KEYS])
        pt_s = o("smp_pt", [P, NPAGE, P])
        ptn_s = o("smp_ptn", [NS, P])

        p = Region(arena, arena_end)
        u_p = p("pool_u", [P, KT, PADW + SEQ])
        u_s = p("pool_u_s", [P, KT, DB, PADW + DQ])
        u_new = p("pool_u_new", [P, KT, NS])
        gate_p = p("pool_gate", [P, KT, TOK])
        d_hi = p("pool_d_hi", [P, KT, TOK], F32R)
        d_lo = p("pool_d_lo", [P, KT, TOK], F32R)
        px = Region(xn_at, xn_end)
        win = px("pool_win", [P, 2, PADW + SEQ])
        win_s = px("pool_win_s", [P, 2, DB, PADW + DQ])
        small_d = px("pool_small", [P, PADW])
        d_tmp = (at("pool_d_tmp", [P, TOK], F32, gain_at), px("pool_d_tmp1", [P, TOK]))
        old_rows = p("pool_old", [DB * STATE, D])
        new_rows = p("pool_rows", [NS, 2, D])

        psum = ctx.enter_context(nc.psum_tensor("psum", [P, NBANK, 512], F32))
        wide = psum[:].rearrange("p b c -> p (b c)")

        items = []

        def f_item(key, w, c0, n, kk=KT):
            items.append((key, w[:, c0:c0 + n].rearrange("(k p) n -> p k n", p=P), kk, n, "w"))

        def t_item(key, w, c0, n, k0, kk):
            items.append((key, w[k0 * P:(k0 + kk) * P, c0:c0 + n].rearrange("(k p) n -> p k n", p=P), kk, n, "w"))

        def t_block(key, w, c0, n):
            for kh in range(2):
                t_item(key + (n, kh), w, c0 + n * BLK, BLK, kh * 4, 4)

        for L, kind in enumerate(KINDS):
            j = L // 3
            if kind == 0:
                w = gla_w_in[j]
                t_block((L, "v"), w, 2 * GH * GDK, 0)
                f_item((L, "a"), w, 2 * GH * GDK + 2 * D, RANK)
                t_block((L, "v"), w, 2 * GH * GDK, 1)
                for x in range(2):
                    f_item((L, "k", x), w, GH * GDK + x * HALF, HALF)
                for x in range(2):
                    f_item((L, "q", x), w, x * HALF, HALF)
                for x in range(4):
                    f_item((L, "g", x), w, 2 * GH * GDK + D + x * HALF, HALF)
                for n in range(2):
                    t_block((L, "out"), gla_w_out[j], 0, n)
            elif kind == 1:
                w = dsa_w_in[j]
                c_iq = 4 * D
                f_item((L, "ikw"), w, c_iq + IH * ID, ID + IH)
                f_item((L, "iq"), w, c_iq, IH * ID)
                t_block((L, "k"), w, D, 0)
                f_item((L, "q", 0), w, 0, HALF)
                t_block((L, "k"), w, D, 1)
                for x in range(1, 4):
                    f_item((L, "q", x), w, x * HALF, HALF)
                for n in range(2):
                    t_block((L, "v"), w, 2 * D, n)
                for x in range(4):
                    f_item((L, "g", x), w, 3 * D + x * HALF, HALF)
                pairs = [[(b, x) for b in range(4 * grp, 4 * grp + 4) for x in range(NPAGE // 2)] for grp in range(2)]
                order = [("K", *pr) for pr in pairs[0]]
                for k_pair, v_pair in zip(pairs[1], pairs[0]):
                    order += [("K", *k_pair), ("V", *v_pair)]
                order += [("V", *pr) for pr in pairs[1]]
                for n, (kv, b, x) in enumerate(order):
                    items.append(((L, kv, b, x), None, 2, D, kv))
                    if n >= len(order) - 3 and n < len(order) - 1:
                        kh = n - (len(order) - 3)
                        t_item((L, "out", 0, kh), dsa_w_out[j], 0, BLK, kh * 4, 4)
                t_block((L, "out"), dsa_w_out[j], 0, 1)
            else:
                w = pool_w_in[j]
                for x in range(4):
                    f_item((L, "u", x), w, x * HALF, HALF)
                for x in range(4):
                    f_item((L, "g", x), w, D + x * HALF, HALF)
                items.append(((L, "grp"), pool_w_grp[j].rearrange("g (k p) n -> p (g k) n", p=P), KT, HALF, "w"))
                for n in range(2):
                    t_block((L, "out"), pool_w_out[j], 0, n)
        index = {it[0]: n for n, it in enumerate(items)}
        weights = [it[0] for it in items if it[4] == "w"]
        pair_of = {key: n for n, key in enumerate(weights)}

        slot, before, held_by = {}, {}, {s: None for s in range(RAW)}
        paged = [it[0] for it in items if it[4] in "KV"]
        for n, it in enumerate(items):
            if it[0] == paged[0]:
                held_by.update({s: items[n - 1][0] for s in range(RAW, RAW + SPARE)})
            wide_choice = it[4] in "KV" and it[0] in paged[:-8]
            s = min(range(RAW + SPARE if wide_choice else RAW),
                    key=lambda x: (-1 if held_by[x] is None else index[held_by[x]], x))
            slot[it[0]], before[it[0]], held_by[s] = s, held_by[s], it[0]
        last_spare = [k for k in paged if slot[k] >= RAW][-1]

        def held(s):
            return raw[:, s, :] if s < RAW else spare[:, s - RAW, :]

        def raw_view(key):
            kk, w = items[index[key]][2:4]
            return held(slot[key])[:, 0:kk * w].rearrange("p (k n) -> p k n", k=kk)

        def pair_view(t, key):
            kk, w = items[index[key]][2:4]
            return t[:, pair_of[key] % 2, 0:kk * w].rearrange("p (k n) -> p k n", k=kk)

        block = ctx.enter_context(nc.Block())

        @block.sync
        def _(sp):
            sp.dma_start(ptab[:], page_table.rearrange("(a b) c -> a (b c)", a=1)).then_inc(*sig("page_table", n=16))

            def tokens_in(t):
                src = x_prompt[0, t * P:(t + 1) * P, :] if t < NP_T else x_sample.rearrange("b q d -> (b q) d")
                sp.dma_start(X[0:rows(t), t, :], src).then_inc(*sig(f"x_in{t}", n=16))

            def norm_gain(L):
                src = [gla_norm[0], dsa_norm[0], pool_norm[0], gla_norm[1], final_norm][L]
                if L:
                    sp.wait_ge(*on("h_lo", (L - 1, "out"), SMP, 1))
                sp.dma_start(gain[:], src.partition_broadcast(P)).then_inc(*sig("gain", L, n=16))

            def small(L):
                j = L // 3
                if KINDS[L] == 0:
                    if j:
                        sp.wait_ge(*on("h_lo", (0, "out"), SMP, 1))
                    sp.dma_start(w_a2[:], gla_w_a2[j]).then_inc(*sig("gla_small", L, 0, n=16))
                    sp.dma_start(b_a[:], gla_b_a[j].rearrange("(h p) -> p h", p=P),
                                 allow_slow_non_contiguous=True).then_inc(*sig("gla_small", L, 1, n=16))
                    sp.dma_start(g_on[:], gla_out_norm[j].partition_broadcast(P)).then_inc(*sig("gla_small", L, n=16))
                if KINDS[L] == 2:
                    sp.dma_start(scale_p[:], pool_scale[j].rearrange("(k p) -> p k", p=P), allow_slow_non_contiguous=True)\
                        .then_inc(*sig("pool_small", n=16))
                    sp.wait_ge(*on("h_lo", (L - 1, "out"), SMP, 1))
                    sp.wait_ge(*on("stores_v", "all"))
                    sp.wait_ge(*on("stores_ik", "all"))
                    for t in range(TILES):
                        sp.wait_ge(*on(f"stores_k{t}", "all"))
                    sp.dma_start(old_rows[:], state_pool[j].rearrange("b r d -> (b r) d"))\
                        .then_inc(*sig("pool_old", n=16))

            def state_load(L, b):
                j = L // 3
                if b >= 3:
                    sp.wait_ge(*on(f"s_stored{b % 3}", L, b - 3))
                elif L:
                    sp.wait_ge(*on("h_lo", (L - 1, "out"), SMP, 1))
                sp.dma_start(s_in[:, b % 3], state_gla[j, b].rearrange("h k v -> k h v"))\
                    .then_inc(*sig(f"s_in{b % 3}", L, b, n=16))

            sp.wait_ge(*on("page_table"))
            tokens_in(0)
            norm_gain(0)
            tokens_in(1)
            for n, (key, src, kk, w, kind) in enumerate(items):
                L = key[0]
                s, old = slot[key], before[key]
                if old is not None:
                    if items[index[old]][4] != "w":
                        sp.wait_ge(*on("pages_used", old))
                    elif s < RAW:
                        sp.wait_ge(*on("split", old))
                    else:
                        sp.wait_ge(*on("proj", ("item", old)))
                if kind == "w":
                    sp.dma_start(raw_view(key), src).then_inc(*sig(f"raw{s}", key, n=16))
                else:
                    cache = cache_k if kind == "K" else cache_v
                    for x in range(2):
                        col = key[2] * NPAGE + key[3] * 2 + x
                        r = sp.value_load(ptab[0:1, col:col + 1], min_val=0, max_val=cache_k.shape[1] - 1)
                        sp.dma_start(held(s)[:, x * D:(x + 1) * D],
                                     cache[0, bass.ds(r, 1)].rearrange("a p h e -> (a p) (h e)"))\
                            .then_inc(*sig(f"raw{s}", key, n=16))
                if n == 0:
                    for t in range(2, TILES):
                        tokens_in(t)
                if n == 1:
                    small(0)
                if KINDS[L] == 0:
                    for b in {(L, "g", 0): (0, 1, 2), (L, "out", 0, 1): (3, 4), (L, "out", 1, 0): (5, 6),
                              (L, "out", 1, 1): (7,)}.get(key, ()):
                        state_load(L, b)
                if key == (L, "k", 0, 1) and KINDS[L] == 1:
                    sp.wait_ge(*on("h_lo", (L - 1, "out"), SMP, 1))
                    for col in range(DB * NPAGE):
                        r = sp.value_load(ptab[0:1, col:col + 1], min_val=0, max_val=cache_k.shape[1] - 1)
                        sp.dma_start(idx_pages[:, col, :], cache_idx_k[0, bass.ds(r, 1)].rearrange("a p n -> (a p) n"))\
                            .then_inc(*sig(f"idx_pages{col // (4 * NPAGE)}", n=16))
                if key == (L, "out", 1, 1):
                    norm_gain(L + 1)
                    if L + 1 < len(KINDS):
                        small(L + 1)
            for name in ("stores_pool", "stores_v", "stores_ik", "stores_gla", "stores_y0", "stores_y1"):
                sp.wait_ge(*on(name, "all"))
            for t in range(TILES):
                sp.wait_ge(*on(f"stores_k{t}", "all"))
            for s in range(3):
                sp.wait_ge(*on(f"s_stored{s}", "all"))

        @block.gpsimd
        def _(pool):
            def select(out, fill, base, pattern, mult, op=ALU.is_ge):
                pool.affine_select(out=out, in_=out, compare_op=op, fill=fill, base=base, pattern=pattern,
                                   channel_multiplier=mult).then_inc(*sig("const"))
                pool.wait_ge(*on_now("const"))

            def fill(out, value):
                pool.memset(out, value).then_inc(*sig("const"))
                pool.wait_ge(*on_now("const"))

            def on_now(name):
                return semaphore(name), count[name]

            fill(ident[:], 0.0)
            select(ident[:], 1.0, 0, [[-1, P]], 1, ALU.not_equal)
            fill(eps[:], RMS_EPS)
            fill(one[:], 1.0)
            plan.value[("const", "first")] = count["const"]

            def other_constants():
                fill(no_reset[:], 1.0)
                fill(no_reset[:, 0:SEQ:CH], 0.0)
                fill(no_reset[:, SEQ:TOK:DQ], 0.0)
                fill(chunk_tri[:], 1.0)
                select(chunk_tri[:], 0.0, 0, [[1, P]], -1)
                fill(chunk_tri[0:CH, CH:P], 0.0)
                fill(seq_tri[:], 1.0)
                select(seq_tri[:], 0.0, 0, [[1, NS]], -1)
                sv = seq_tri[:].rearrange("p (b q) -> p b q", b=DB)
                select(sv, 0.0, 0, [[-DQ, DB], [0, DQ]], 1)
                fill(future_p[:], 0.0)
                select(future_p[:], FUTURE, 0, [[-1, P]], 1)
                fill(future_s[:], 0.0)
                select(future_s[:], FUTURE, 0, [[-1, NS]], 1)
                fv = future_s[:].rearrange("p (b q) -> p b q", b=DB)
                select(fv, FUTURE, DQ - 1, [[DQ, DB], [0, DQ]], -1)
                fill(stack4[:], 0.0)
                for h in range(IH):
                    select(stack4[:], 1.0, -NS * h, [[-1, NS]], 1, ALU.not_equal)
                fill(pick_tok[:], 0.0)
                pv = pick_tok[:].rearrange("p b (h q) -> p b h q", q=DQ)
                select(pv, 1.0, 0, [[-DQ, DB], [0, DH], [-1, DQ]], 1, ALU.not_equal)
                fill(seq_col[:], 1.0)
                select(seq_col[:], 0.0, 0, [[-DQ, DB], [1, NS]], 0)
                select(seq_col[:], 0.0, DQ - 1, [[DQ, DB], [-1, NS]], 0)
                fill(seq_row[:], 1.0)
                select(seq_row[:], 0.0, 0, [[-DQ, DB]], 1)
                select(seq_row[:], 0.0, DQ - 1, [[DQ, DB]], -1)
                pool.iota(cnt_i[:].bitcast(I32), pattern=[[1, PADW]], base=1, channel_multiplier=0)\
                    .then_inc(*sig("const"))
                pool.wait_ge(*on_now("const"))
                pool.tensor_copy(inv_cnt[:], cnt_i[:].bitcast(I32)).then_inc(*sig("const"))

            for n, key in enumerate(weights):
                if n == 2:
                    other_constants()
                s = slot[key]
                pool.wait_ge(*on(f"raw{s}", key))
                if key == (last_spare[0], "out", 0, 0):
                    pool.wait_ge(*on("pages_used", last_spare))
                if n >= 2:
                    pool.wait_ge(*on("proj", ("item", weights[n - 2])))
                pool.tensor_tensor(pair_view(w_hi, key), raw_view(key), one[:].unsqueeze(1).broadcast_to(
                    [P, *raw_view(key).shape[1:]]), ALU.mult)\
                    .then_inc(*sig("split_hi", key))
                pool.wait_ge(*on("split_hi", key))
                pool.tensor_tensor(pair_view(w_lo, key), raw_view(key), pair_view(w_hi, key).bitcast(F32),
                                   ALU.subtract).then_inc(*sig("split", key))

        @block.tensor
        def _(pe):
            reader = {}

            def claim(b, key, last):
                if b in reader:
                    pe.wait_ge(*on(*reader[b]))
                reader[b] = last
                plan.bank[key] = b
                return b

            turn = {}

            def next_bank(banks=range(NBANK)):
                banks = tuple(banks)
                turn[banks] = turn.get(banks, 0) + 1
                return banks[turn[banks] % len(banks)]

            def product(out, lh, ll, rh, rl, start, stop):
                pe.matmul(out, lh, rh, start=start, stop=False)
                pe.matmul(out, lh, rl, start=False, stop=False)
                return pe.matmul(out, ll, rh, start=False, stop=stop)

            def norm_in(L, tiles, banks=range(NBANK)):
                for t in tiles:
                    pe.wait_ge(*on("xn", L, t))
                    for half in range(2):
                        b = claim(next_bank(banks), ("nT", L, t, half), ("h_lo", L, t, half))
                        for k in range(4):
                            mm = pe.transpose(psum[:, b, k * P:k * P + rows(t)],
                                              xn[0:rows(t), t % 2, (4 * half + k) * P:(4 * half + k + 1) * P],
                                              ident[0:rows(t), 0:rows(t)])
                        mm.then_inc(*sig("nT", L, t, half))

            def wait_h(tag, tiles):
                for t in tiles:
                    pe.wait_ge(*on("h_lo", tag, t, 1))

            def part_job(name, m, reader_name, banks, lhs, rhs, kk, items_done=(), between=None):
                for part, c in PARTS:
                    b = claim(banks[part] if len(banks) == 2 else next_bank(banks), ("proj", name, part),
                              (reader_name, name, part))
                    for k in range(kk):
                        mm = product(psum[0:m, b, 0:HC], *lhs(k), *rhs(k, c), k == 0, k == kk - 1)
                    mm.then_inc(*sig("proj", name, part, also=items_done if part else ()))
                    if between and part == 0:
                        between()

            def h_pair(k, c):
                return h_hi[:, k, c], h_lo[:, k, c]

            def f_job(key, jobs, reader_name, banks, between=None):
                wh, wl = pair_view(w_hi, key), pair_view(w_lo, key)
                pe.wait_ge(*on("split", key))
                for x, (name, c0, m) in enumerate(jobs):
                    part_job(name, m, reader_name, banks, lambda k: (wh[:, k, c0:c0 + m], wl[:, k, c0:c0 + m]),
                             h_pair, KT, ((("item", key),),) if x == len(jobs) - 1 else (),
                             between if x == 0 else None)

            def last_norms(L):
                norm_in(L, (3, SMP))
                wait_h(L, (3, SMP))

            def t_job(keys, name, n, reader_name, banks, tag, before_tile=None, after_tile=None):
                bs, k0 = [], 0
                for x, key in enumerate(keys):
                    wh, wl = pair_view(w_hi, key), pair_view(w_lo, key)
                    kk = items[index[key]][2]
                    pe.wait_ge(*on("split", key))
                    for t in range(TILES):
                        if x == 0 and before_tile:
                            before_tile(t)
                        if x == 0:
                            pe.wait_ge(*on("h_lo", tag, t, 1))
                            bs.append(claim(next_bank(banks), ("proj", name, t), (reader_name, name, t)))
                        for k in range(kk):
                            mm = product(psum[0:rows(t), bs[t], 0:n], h_hi[:, k0 + k, cols(t)],
                                         h_lo[:, k0 + k, cols(t)], wh[:, k, :], wl[:, k, :],
                                         k0 + k == 0, k0 + k == KT - 1)
                        last_t = ((("item", key),),) if t == TILES - 1 else ()
                        if x == len(keys) - 1:
                            mm.then_inc(*sig("proj", (name, t), also=last_t))
                            if after_tile:
                                after_tile(t)
                        elif t == TILES - 1:
                            mm.then_inc(*sig("proj", ("item", key)))
                    k0 += kk

            def out_proj(L):
                def next_norm(t):
                    if t >= 2 and L + 1 < len(KINDS):
                        norm_in(L + 1, [t - 2])

                for n in range(2):
                    t_job([(L, "out", n, kh) for kh in range(2)], (L, "out", n), BLK, "resid", range(NBANK),
                          (L, "out"), after_tile=next_norm if n else None)

            def out_transposes(L, t, source, ready):
                pe.wait_ge(*on(*ready))
                for half in range(2):
                    b = claim(next_bank(), ("oT", L, t, half), ("oT_read", L, t, half))
                    for k in range(4):
                        kt = 4 * half + k
                        mm = pe.transpose(psum[:, b, k * P:k * P + rows(t)],
                                          source[0:rows(t), t, kt * P:(kt + 1) * P], ident[0:rows(t), 0:rows(t)])
                    mm.then_inc(*sig("oT", L, t, half))

            def gla(L):
                def norm_ahead(t):
                    if L == 0:
                        if 1 <= t < TILES - 1:
                            norm_in(L, [t + 1], (5, 6, 7))
                    elif t in (1, 2):
                        norm_in(L, [t + 2], (5, 6, 7))

                if L == 0:
                    norm_in(L, [0, 1], (5, 6, 7))
                t_job([(L, "v", 0, kh) for kh in range(2)], (L, "v", 0), BLK, "v", range(5), L, norm_ahead)
                f_job((L, "a"), [((L, "a"), 0, RANK)], "a", range(NBANK))
                pe.wait_ge(*on("a", (L, "a"), 1))
                pe.wait_ge(*on("gla_small", L))
                bs = claim(next_bank(), ("z", L, "s"), ("z_read", L, "s"))
                for h in range(GH):
                    b = claim(next_bank(), ("z", L, h), ("z_read", L, h))
                    w = w_a2[:, h * GDK:(h + 1) * GDK]
                    pe.matmul(psum[:, b, 0:SEQ], w, a_t[:, 0:SEQ], start=True, stop=True).then_inc(*sig("z", L, h))
                    mm = pe.matmul(psum[:, bs, h * NS:(h + 1) * NS], w, a_t[:, SEQ:TOK], start=True, stop=True)
                mm.then_inc(*sig("z", L, "s"))
                t_job([(L, "v", 1, kh) for kh in range(2)], (L, "v", 1), BLK, "v", range(NBANK), L)
                for x in range(2):
                    f_job((L, "k", x), [((L, "k", 2 * x + y), y * P, P) for y in range(2)], "k_gated", range(NBANK))
                for x in range(2):
                    f_job((L, "q", x), [((L, "q", 2 * x + y), y * P, P) for y in range(2)], "q_gated", range(NBANK))
                pe.wait_ge(*on("k_gated", (L, "k", GH - 1), 1))
                for t in range(TILES):
                    b = claim(next_bank(), ("kT", L, t), ("k_tok", L, t))
                    for h in range(GH):
                        mm = pe.transpose(psum[0:rows(t), b, h * P:(h + 1) * P], kg[:, h, cols(t)], ident[:])
                    mm.then_inc(*sig("kT", L, t))
                pe.wait_ge(*on("q_gated", (L, "q", GH - 1), 1))
                pe.wait_ge(*on("v", (L, "v", 1), SMP))

                def states(c):
                    r = slice((c % 2) * CH, (c % 2) * CH + CH)
                    for half in range(2):
                        claim(1 + half, ("state", L, c, half), ("s_sum", L, c))
                    for h in range(GH):
                        mm = pe.matmul(psum[:, 1 + h // 2, (h % 2) * GDV:(h % 2 + 1) * GDV],
                                       k_tok[r, c // 2, h * GDK:(h + 1) * GDK],
                                       v_g[r, c // 2, h * GDV:(h + 1) * GDV], start=True, stop=True)
                    mm.then_inc(*sig("state", L, c))

                def carried(c, last):
                    r = (c % 2) * CH
                    if c:
                        pe.wait_ge(*on("s_now", L, c))
                    for h in range(GH):
                        if c:
                            mm = pe.matmul(psum[r:r + CH, 3 + h // 2, (h % 2) * GDV:(h % 2 + 1) * GDV],
                                           qg[:, h, c * CH:(c + 1) * CH], s_now[:, c % 2, h * GDV:(h + 1) * GDV],
                                           start=False, stop=last and h % 2 == 1, skip_group_check=True)
                    if last:
                        mm.then_inc(*sig("o", L, c // 2))

                g_jobs = [((L, "g", 2 * x + y), (L, "g", x), y) for x in range(4) for y in range(2)]

                def g_job(n):
                    name, key, y = g_jobs[n]
                    if y == 0:
                        pe.wait_ge(*on("split", key))
                    wh, wl = pair_view(w_hi, key), pair_view(w_lo, key)
                    part_job(name, P, "gate", (5, 6),
                             lambda k: (wh[:, k, y * P:(y + 1) * P], wl[:, k, y * P:(y + 1) * P]), h_pair, KT,
                             ((("item", key),),) if y else (), lambda: sequence(n))

                def out_s(h):
                    return psum[(h // 2) * NS:(h // 2 + 1) * NS, 7, (h % 2) * GDV:(h % 2 + 1) * GDV]

                claim(0, ("att", L, SMP), ("att_m", L, SMP))
                for h in range(GH):
                    mm = pe.matmul(psum[0:NS, 0, h * NS:(h + 1) * NS], kg[:, h, SEQ:TOK], qg[:, h, SEQ:TOK],
                                   start=True, stop=True)
                mm.then_inc(*sig("att", L, SMP))
                pe.wait_ge(*on("att_m", L, SMP))
                claim(7, ("o", L, SMP, 0), ("o_out", L, SMP))
                for h in range(GH):
                    pe.matmul(out_s(h), att_g[0:NS, h, 0:NS], v_g[0:NS, SMP, h * GDV:(h + 1) * GDV],
                              start=h % 2 == 0, stop=False, skip_group_check=True)
                pe.wait_ge(*on("q_seq", L))

                def sequence(b):
                    pe.wait_ge(*on(f"s_in{b % 3}", L, b))
                    for h in range(GH):
                        mm = pe.matmul(out_s(h), q_seq[:, h, b, :], s_in[:, b % 3, h, :], start=False,
                                       stop=b == DB - 1 and h % 2 == 1, skip_group_check=True)
                    if b == DB - 1:
                        mm.then_inc(*sig("o", L, SMP))
                    pe.wait_ge(*on("k_seq", L, b))
                    for half in range(2):
                        claim(1 + half, ("s_state", L, b, half), ("s_new", L, b))
                    for h in range(GH):
                        mm = pe.matmul(psum[:, 1 + h // 2, (h % 2) * GDV:(h % 2 + 1) * GDV],
                                       k_seq[:, b % 2, h * GDK:(h + 1) * GDK],
                                       v_g[0:NS, SMP, h * GDV:(h + 1) * GDV], start=True, stop=True)
                    mm.then_inc(*sig("s_state", L, b))

                for t in range(NP_T):
                    claim(0, ("att", L, t), ("att_m", L, t))
                    for h in range(GH):
                        mm = pe.matmul(psum[:, 0, h * P:(h + 1) * P], kg[:, h, cols(t)], qg[:, h, cols(t)],
                                       start=True, stop=True)
                    mm.then_inc(*sig("att", L, t))
                    pe.wait_ge(*on("k_tok", L, t))
                    states(2 * t)
                    g_job(2 * t)
                    pe.wait_ge(*on("att_m", L, t))
                    for half in range(2):
                        claim(3 + half, ("o", L, t, half), ("o_out", L, t))
                    for h in range(GH):
                        pe.matmul(psum[:, 3 + h // 2, (h % 2) * GDV:(h % 2 + 1) * GDV], att_g[:, h, :],
                                  v_g[:, t, h * GDV:(h + 1) * GDV], start=h % 2 == 0, stop=False,
                                  skip_group_check=True)
                    carried(2 * t, False)
                    states(2 * t + 1)
                    g_job(2 * t + 1)
                    carried(2 * t + 1, True)

                for t in range(TILES):
                    out_transposes(L, t, v_g, ("o_norm", L, t))
                out_proj(L)

            def dsa(L):
                wait_h(L, range(3))
                f_job((L, "ikw"), [((L, "ikw"), 0, ID + IH)], "ik", range(NBANK), lambda: last_norms(L))
                f_job((L, "iq"), [((L, "iq", y), y * P, P) for y in range(2)], "iq", range(NBANK))
                pe.wait_ge(*on("ik", (L, "ikw"), 1))
                for x, tiles in enumerate((range(NP_T), (SMP,))):
                    b = claim(next_bank(), ("ikwT", L, x), ("ikw", L, x))
                    for t in tiles:
                        mm = pe.transpose(psum[0:rows(t), b, (t % 4) * P:(t % 4) * P + ID + IH], ik[:, cols(t)],
                                          ident[0:ID + IH, 0:ID + IH])
                    mm.then_inc(*sig("ikwT", L, x))
                pe.wait_ge(*on("iq", (L, "iq", 1), 1))
                for t in range(1, NP_T):
                    for h in range(IH):
                        b = claim(next_bank(), ("idx", L, t, h), ("idx_relu", L, t, h))
                        pe.matmul(psum[:, b, 0:(t + 1) * P], iq[:, h, cols(t)], ik[0:ID, 0:(t + 1) * P],
                                  start=True, stop=True).then_inc(*sig("idx", L, t, h))
                t_job([(L, "k", 0, kh) for kh in range(2)], (L, "k", 0), BLK, "k_st", range(NBANK), L)
                pe.wait_ge(*on("iq_seq", L))
                steps = [(c, b) for c in range(2) for b in range(DB)]

                def turn_old(c, b):
                    if b % 4 == 0:
                        pe.wait_ge(*on(f"idx_pages{b // 4}", "all"))
                    kb = claim((3, 4)[b % 2], ("oldT", L, c, b), ("ik_old", L, c, b))
                    for pg in range(4):
                        mm = pe.transpose(psum[0:ID, kb, pg * P:(pg + 1) * P], idx_pages[:, b * NPAGE + 4 * c + pg, :],
                                          ident[:])
                    mm.then_inc(*sig("idx_turned", L, c, b))

                turn_old(*steps[0])
                for i, (c, b) in enumerate(steps):
                    if i + 1 < len(steps):
                        turn_old(*steps[i + 1])
                    if b == 0:
                        claim(c, ("idx_s", L, c), ("idx_relu_s", L, c))
                    pe.wait_ge(*on("ik_old", L, c, b))
                    for h in range(IH):
                        mm = pe.matmul(psum[h * NS:(h + 1) * NS, c, :], iq_seq[:, h, b, :], ik_old[:, b % 2, :],
                                       start=b == 0, stop=b == DB - 1)
                    mm.then_inc(*sig("idx_s", L, c, b, also=(((L, c),) if b == DB - 1 else ())))
                claim(2, ("idx_s", L, 2), ("idx_relu_s", L, 2))
                for h in range(IH):
                    mm = pe.matmul(psum[h * NS:(h + 1) * NS, 2, 0:NS], iq[:, h, SEQ:TOK], ik[0:ID, SEQ:TOK],
                                   start=True, stop=True)
                mm.then_inc(*sig("idx_s", L, 2))
                pe.wait_ge(*on("w_sel", L))
                for c, w in enumerate((BLK, BLK, NS)):
                    pe.wait_ge(*on("idx_relu_s", L, c))
                    b = claim(5 + c, ("score_s", L, c), ("score_s", L, c))
                    pe.matmul(psum[0:NS, b, 0:w], w_sel[:], relu_s[:, c * BLK:c * BLK + w], start=True, stop=True)\
                        .then_inc(*sig("score_mm", L, c))

                def k_transposes(n):
                    for t in range(TILES):
                        pe.wait_ge(*on("k_st", (L, "k", n), t))
                        b = claim(next_bank(), ("dkT", L, n, t), ("k_d", L, n, t))
                        for h in range(4):
                            mm = pe.transpose(psum[:, b, h * P:h * P + rows(t)], k_st[0:rows(t), t, h * P:(h + 1) * P],
                                              ident[0:rows(t), 0:rows(t)])
                        mm.then_inc(*sig("dkT", L, n, t))

                f_job((L, "q", 0), [((L, "q", y), y * P, P) for y in range(2)], "q_d", range(NBANK))
                k_transposes(0)
                t_job([(L, "k", 1, kh) for kh in range(2)], (L, "k", 1), BLK, "k_st", range(NBANK), L)
                for x in range(1, 4):
                    f_job((L, "q", x), [((L, "q", 2 * x + y), y * P, P) for y in range(2)], "q_d", range(NBANK))
                    if x == 1:
                        k_transposes(1)
                for n in range(2):
                    t_job([(L, "v", n, kh) for kh in range(2)], (L, "v", n), BLK, "v_d", range(NBANK), L)
                for x in range(4):
                    f_job((L, "g", x), [((L, "g", 2 * x + y), y * P, P) for y in range(2)], "gate", range(NBANK))

                pe.wait_ge(*on("q_d", (L, "q", DH - 1), 1))
                pe.wait_ge(*on("k_d", L, 1, SMP))
                pe.wait_ge(*on("v_d", (L, "v", 1), SMP))
                units = [(t, h) for t in range(NP_T) for h in range(DH)]

                def scores(n):
                    t, h = units[n]
                    b = claim((0, 1, 7)[n % 3], ("S", L, n), ("S_read", L, n))
                    pe.matmul(psum[:, b, 0:(t + 1) * P], q_d[:, h, cols(t)], k_d[:, h, 0:(t + 1) * P],
                              start=True, stop=True).then_inc(*sig("S", L, n))

                def probs(n):
                    t, h = units[n]
                    b = claim((2, 3, 6)[n % 3], ("PT", L, n), ("PT_read", L, n))
                    pe.wait_ge(*on("p_norm", L, n))
                    for s in range(t + 1):
                        mm = pe.transpose(psum[:, b, s * P:(s + 1) * P], p_at[:, n % 3, s * P:(s + 1) * P], ident[:])
                    mm.then_inc(*sig("PT", L, n))

                def values(n):
                    t, h = units[n]
                    m = n // 4
                    if n % 4 == 0:
                        claim((4, 5)[m % 2], ("O", L, m), ("oT_read", L, t, h // 4))
                    b = (4, 5)[m % 2]
                    pe.wait_ge(*on("PT_read", L, n))
                    for s in range(t + 1):
                        mm = pe.matmul(psum[:, b, (h % 4) * P:(h % 4 + 1) * P], v_d[:, s, h * HD:(h + 1) * HD],
                                       pt_at[:, n % 2, s * P:(s + 1) * P], start=s == 0, stop=s == t)
                    mm.then_inc(*sig("O", L, n))

                N = len(units)
                for n in range(N + 3):
                    if n < N:
                        scores(n)
                    if 2 <= n <= N + 1:
                        probs(n - 2)
                    if n >= 3:
                        values(n - 3)

                pe.wait_ge(*on("bias_s", L))
                halves = [(b, pg, half) for b in range(DB) for pg in range(NPAGE) for half in range(2)]

                def turn_keys(i):
                    b, pg, half = halves[i]
                    key = (L, "K", b, pg // 2)
                    s = slot[key]
                    if pg % 2 == 0 and half == 0:
                        pe.wait_ge(*on(f"raw{s}", key))
                    kb = claim(5 + i % 3, ("KT", L, i), (f"kt_s{half}", L, i))
                    for h in range(4):
                        o = (pg % 2) * D + (4 * half + h) * HD
                        mm = pe.transpose(psum[:, kb, h * P:(h + 1) * P], held(s)[:, o:o + HD], ident[:])
                    mm.then_inc(*sig("pages_used", L, "kT", i, also=((key,),) if pg % 2 and half else ()))

                def key_scores(i):
                    b, pg, half = halves[i]
                    grp, bl = b // 4, b % 4
                    r = slice(bl * NS, (bl + 1) * NS)
                    if bl == 0 and pg == 0 and half == 0:
                        for x in range(3):
                            claim(x, ("SS", L, grp, x), ("ss_read", L, grp))
                    if i == 0:
                        pe.wait_ge(*on("q_heads", L))
                    c = pg * PAGE
                    out = psum[r, c // BLK, c % BLK:c % BLK + PAGE]
                    if half == 0:
                        pe.matmul(out, pick_tok[:, b, :], bias_s[:, c:c + PAGE], start=True, stop=False)
                    pe.wait_ge(*on(f"kt_s{half}", L, i))
                    for h in range(4 * half, 4 * half + 4):
                        mm = pe.matmul(out, q_heads[:, h, b, :], kt_s[:, (i // 2) % 2, h, :], start=False,
                                       stop=h == DH - 1)
                    mm.then_inc(*sig("key_scores", L, i))
                    if pg == NPAGE - 1 and half:
                        out = psum[r, 2, 0:NS]
                        pe.matmul(out, pick_tok[:, b, :], bias_s[:, PAST:KEYS], start=True, stop=False)
                        for h in range(DH):
                            mm = pe.matmul(out, q_heads[:, h, b, :], ks_d[:, h, :], start=False, stop=h == DH - 1)
                        if bl == 3:
                            mm.then_inc(*sig("SS", L, grp))

                def turn_probs(grp):
                    pe.wait_ge(*on("ps_norm", L, grp))
                    for x in range(3):
                        b = claim(5 + x, ("PsT", L, grp, x), ("pt_s", L, grp, x))
                        if x < 2:
                            for pg in range(4):
                                o = (4 * x + pg) * PAGE
                                mm = pe.transpose(psum[:, b, pg * P:(pg + 1) * P], p_s[:, o:o + PAGE], ident[:])
                        else:
                            mm = pe.transpose(psum[0:NS, b, 0:P], p_s[:, PAST:KEYS], ident[:])
                        mm.then_inc(*sig("PsT", L, grp, x))
                    pe.wait_ge(*on("pt_s", L, grp, 2))
                    for half in range(2):
                        claim(3 + half, ("Os", L, grp, half), (f"o_full{half}", L, grp))

                def value_pair(n):
                    b, x = n // (NPAGE // 2), n % (NPAGE // 2)
                    bl = b % 4
                    r = slice(bl * NS, (bl + 1) * NS)
                    key = (L, "V", b, x)
                    s = slot[key]
                    pe.wait_ge(*on(f"raw{s}", key))
                    for y in range(2):
                        for half in range(2):
                            o = y * D + half * BLK
                            mm = pe.matmul(psum[r, 3 + half, :], pt_s[:, 2 * x + y, r], held(s)[:, o:o + BLK],
                                           start=x == 0 and y == 0, stop=False)
                    mm.then_inc(*sig("pages_used", key))
                    if x == NPAGE // 2 - 1:
                        for half in range(2):
                            mm = pe.matmul(psum[r, 3 + half, :], ptn_s[:, r], v_d[0:NS, SMP, half * BLK:(half + 1) * BLK],
                                           start=False, stop=True)
                        if bl == 3:
                            mm.then_inc(*sig("Os", L, b // 4))

                def turn_out(grp):
                    for half in range(2):
                        pe.wait_ge(*on(f"o_full{half}", L, grp))
                        b = claim(5 + half, ("OsT", L, grp, half), ("os_read", L, grp, half))
                        for h in range(4):
                            o = (4 * half + h) * HD
                            mm = pe.transpose(psum[:, b, h * P:(h + 1) * P], p_s[:, o:o + HD], ident[:])
                        mm.then_inc(*sig("OsT", L, grp, half))

                n_half = len(halves)
                for i in range(n_half + 2):
                    if i < n_half:
                        turn_keys(i)
                    if i >= 2:
                        key_scores(i - 2)
                    if n_half // 2 <= i < n_half and i % 4 == 3:
                        n = (i - n_half // 2) // 4
                        if n == 0:
                            turn_probs(0)
                        value_pair(n)
                turn_out(0)
                turn_probs(1)
                for n in range(16, 32):
                    value_pair(n)
                turn_out(1)
                out_proj(L)

            def pooling(L):
                pe.wait_ge(*on("pool_old"))
                for half in range(2):
                    b = claim(next_bank(), ("oldP", L, half), ("u_old", L, half))
                    for k in range(4):
                        mm = pe.transpose(psum[:, b, k * P:k * P + DB * STATE],
                                          old_rows[:, (4 * half + k) * P:(4 * half + k + 1) * P],
                                          ident[0:DB * STATE, 0:DB * STATE])
                    mm.then_inc(*sig("oldP", L, half))
                wait_h(L, range(3))
                for x in range(4):
                    f_job((L, "u", x), [((L, "u", 2 * x + y), y * P, P) for y in range(2)], "u", range(NBANK),
                          (lambda: last_norms(L)) if x == 0 else None)
                for x in range(4):
                    f_job((L, "g", x), [((L, "g", 2 * x + y), y * P, P) for y in range(2)], "gate", range(NBANK))
                pe.wait_ge(*on("u", (L, "u", KT - 1), 1))
                for part, m in ((0, STATE), (1, NS)):
                    for half in range(2):
                        b = claim(next_bank(), ("rowsT", L, part, half), ("pool_rows", L, part, half))
                        for k in range(4):
                            kt = 4 * half + k
                            src = u_p[:, kt, PADW + SEQ - STATE:] if part == 0 else u_new[:, kt, :]
                            mm = pe.transpose(psum[0:m, b, k * P:(k + 1) * P], src, ident[:])
                        mm.then_inc(*sig("rowsT", L, part, half))
                key = (L, "grp")
                pe.wait_ge(*on("split", key))
                wh, wl = pair_view(w_hi, key), pair_view(w_lo, key)
                for grp in range(len(WINDOWS)):
                    pe.wait_ge(*on("d_lo", L, 2 * grp + 1))
                    for y in range(2):
                        name = (L, "y", 2 * grp + y)
                        part_job(name, P, "y_read", range(NBANK),
                                 lambda k: (wh[:, 2 * grp + k, y * P:(y + 1) * P],
                                            wl[:, 2 * grp + k, y * P:(y + 1) * P]),
                                 lambda k, c: (d_hi[:, 2 * grp + k, c], d_lo[:, 2 * grp + k, c]), 2,
                                 ((("item", key),),) if grp == 3 and y else ())
                out_proj(L)

            pe.wait_ge(*on("const", "first"))
            for L, kind in enumerate(KINDS):
                (gla, dsa, pooling)[kind](L)

        @block.scalar
        def _(act):
            def copy(out, in_, scale=1.0):
                return act.activation(out, in_, ACT.Copy, scale=scale)

            def rstd_guess(sq, ln, y, n_inv, key):
                act.activation(ln, sq, ACT.Ln, bias=eps[0:ln.shape[0], :], scale=n_inv).then_inc(*sig("rstd_ln", *key))
                act.wait_ge(*on("rstd_ln", *key))
                act.activation(y, ln, ACT.Exp, scale=-0.5).then_inc(*sig("rstd_y", *key))

            def norm_hi(L, t):
                r = rows(t)
                for half in range(2):
                    act.wait_ge(*on("nT", L, t, half))
                    b = bank_of("nT", L, t, half)
                    copy(h_hi[:, 4 * half:4 * half + 4, cols(t)],
                         psum[:, b, :].rearrange("p (k t) -> p k t", k=4)[:, :, 0:r])\
                        .then_inc(*sig("h_hi", L, t, half))

            def norm(L, last=False):
                for t in range(TILES):
                    r = rows(t)
                    if L:
                        act.wait_ge(*on("resid", (L - 1, "out", 1), t))
                    else:
                        act.wait_ge(*on(f"x_in{t}"))
                    if t >= 2:
                        act.wait_ge(*on("xn", L, t - 2))
                    s = st[0:r, t % 2, :]
                    act.activation(sq_junk[0:r, :], X[0:r, t, :], ACT.Square, accum_out=s[:, 0:1])\
                        .then_inc(*sig("sumsq", L, t))
                    act.wait_ge(*on("sumsq", L, t))
                    rstd_guess(s[:, 0:1], s[:, 2:3], s[:, 3:4], 1.0 / D, (L, t))
                    if t and not last:
                        norm_hi(L, t - 1)
                    if last:
                        act.wait_ge(*on("xn", L, t))
                        dst = y_prompt[0, t * P:(t + 1) * P, :] if t < NP_T else y_sample.rearrange("b q d -> (b q) d")
                        act.dma_start(dst, xn[0:r, t % 2, :]).then_inc(*sig(f"stores_y{t % 2}", t, n=16))
                if not last:
                    norm_hi(L, SMP)

            def out_hi(L, t, half):
                act.wait_ge(*on("oT_read", L, t, half))
                n = rows(t)
                copy(h_hi[:, 4 * half:4 * half + 4, cols(t)],
                     tmp_og[:, half, 0:4 * n].rearrange("p (k t) -> p k t", k=4))\
                    .then_inc(*sig("h_hi", (L, "out"), t, half))

            def f_out(name, out, mark, fn=ACT.Copy, sample=None):
                m = out.shape[0]
                pieces = [(0, slice(0, HC), out[:, 0:HC])]
                if sample is None:
                    pieces += [(1, slice(0, HC), out[:, HC:TOK])]
                else:
                    pieces += [(1, slice(0, SEQ - HC), out[:, HC:SEQ]), (1, slice(SEQ - HC, HC), sample)]
                for part, c, dst in pieces:
                    act.wait_ge(*on("proj", name, part))
                    act.activation(dst, psum[0:m, bank_of("proj", name, part), c], fn).then_inc(*sig(mark, name, part))

            def t_out(name, t, out, mark):
                act.wait_ge(*on("proj", (name, t)))
                copy(out, psum[0:rows(t), bank_of("proj", name, t), 0:out.shape[-1]]).then_inc(*sig(mark, name, t))

            def gate(L, buf, k):
                f_out((L, "g", k), buf[:, k, :], "gate", ACT.Silu)

            def gla(L):
                j = L // 3
                norm(L)
                if L:
                    act.wait_ge(*on("stores_pool", "all"))
                for t in range(TILES):
                    t_out((L, "v", 0), t, v_g[0:rows(t), t, 0:BLK], "v")
                f_out((L, "a"), a_t[:], "a")
                act.wait_ge(*on("gla_small", L))
                for h in range(GH):
                    act.wait_ge(*on("z", L, h))
                    act.activation(soft[:, h, 0:SEQ], psum[:, bank_of("z", L, h), :], ACT.Abs,
                                   bias=b_a[:, h:h + 1]).then_inc(*sig("z_abs", L, h))
                act.wait_ge(*on("z", L, "s"))
                for h in range(GH):
                    act.activation(soft[:, h, SEQ:TOK], psum[:, bank_of("z", L, "s"), h * NS:(h + 1) * NS], ACT.Abs,
                                   bias=b_a[:, h:h + 1]).then_inc(*sig("z_abs", L, "s"))
                act.wait_ge(*on("z_abs", L, "s"))
                act.activation(soft[:], soft[:], ACT.Exp, scale=-1.0).then_inc(*sig("z_exp", L))
                act.wait_ge(*on("z_exp", L))
                act.activation(soft[:], soft[:], ACT.Ln, bias=one[:]).then_inc(*sig("z_soft", L))
                act.wait_ge(*on("decay", L))
                act.activation(kg[:], qg[:], ACT.Exp, scale=-1.0 / TAU).then_inc(*sig("k_decay", L))
                act.wait_ge(*on("k_decay", L))
                act.activation(qg[:], qg[:], ACT.Exp, scale=1.0 / TAU).then_inc(*sig("q_decay", L))
                act.wait_ge(*on("fac", L))
                act.activation(fac[:], fac[:], ACT.Exp, scale=1.0 / TAU).then_inc(*sig("fac_exp", L))
                for t in range(TILES):
                    t_out((L, "v", 1), t, v_g[0:rows(t), t, BLK:D], "v")
                for t in range(TILES):
                    act.wait_ge(*on("kT", L, t))
                    copy(k_tok[0:rows(t), t, :], psum[0:rows(t), bank_of("kT", L, t), :]).then_inc(*sig("k_tok", L, t))
                act.wait_ge(*on("fac_exp", L))

                def next_state(c):
                    act.wait_ge(*on("s_sum", L, c - 1))
                    if c % 2 and c > 1:
                        act.wait_ge(*on("o", L, c // 2 - 1))
                    for h in range(GH):
                        copy(s_now[:, c % 2, h * GDV:(h + 1) * GDV], s_sum[:, h * GDV:(h + 1) * GDV],
                             fac[:, h, c - 1:c]).then_inc(*sig("s_now", L, c))

                def squares(t):
                    r = rows(t)
                    act.wait_ge(*on("o_out", L, t))
                    if t:
                        act.wait_ge(*on("o_sq", L, t - 1))
                    for h in range(GH):
                        act.activation(sq_junk[0:r, h * GDV:(h + 1) * GDV], v_g[0:r, t, h * GDV:(h + 1) * GDV], ACT.Square,
                                       accum_out=ost[0:r, 0, 4 * t + h:4 * t + h + 1])\
                            .then_inc(*sig("o_sq", L, t))

                def sequence(b):
                    act.wait_ge(*on("s_new", L, b))
                    for h in range(GH):
                        copy(s_in[:, b % 3, h, :], s_in[:, b % 3, h, :], fac[:, h, NCH + b:NCH + b + 1])\
                            .then_inc(*sig("s_end", L, b))
                    act.wait_ge(*on("s_end", L, b))
                    act.dma_start(gla_state_sample[j, b].rearrange("h k v -> k h v"), s_in[:, b % 3])\
                        .then_inc(*sig(f"s_stored{b % 3}", L, b, n=16))

                for t in range(NP_T):
                    next_state(2 * t + 1)
                    if t:
                        squares(t - 1)
                    gate(L, gate_g, 2 * t)
                    sequence(2 * t)
                    next_state(2 * t + 2)
                    gate(L, gate_g, 2 * t + 1)
                    if t < NP_T - 1:
                        sequence(2 * t + 1)
                act.preload_act_table_set(EXP_LN)
                act.wait_ge(*on("o_sq", L, NP_T - 2))
                rstd_guess(ost[:, 0, 0:12], ost[:, 2, 0:12], ost[:, 3, 0:12], 1.0 / GDV, (L, "o", 0))
                squares(NP_T - 1)
                act.wait_ge(*on("o_sq", L, NP_T - 1))
                rstd_guess(ost[:, 0, 12:16], ost[:, 2, 12:16], ost[:, 3, 12:16], 1.0 / GDV, (L, "o", 2))
                act.wait_ge(*on("s_now", L, NCH))
                act.dma_start(gla_state_prompt[j, 0].rearrange("h k v -> k h v"),
                              s_now[:, 0, :].rearrange("p (h v) -> p h v", h=GH)).then_inc(*sig("stores_gla", L, n=16))
                sequence(DB - 1)
                squares(SMP)
                act.wait_ge(*on("o_sq", L, SMP))
                rstd_guess(ost[0:NS, 0, 16:20], ost[0:NS, 2, 16:20], ost[0:NS, 3, 16:20], 1.0 / GDV, (L, "o", 1))
                for t in range(TILES):
                    for half in range(2):
                        out_hi(L, t, half)

            def dsa(L):
                norm(L)
                for s in range(3):
                    act.wait_ge(*on(f"s_stored{s}", L - 1, max(b for b in range(DB) if b % 3 == s)))
                act.wait_ge(*on("stores_gla", L - 1))
                f_out((L, "ikw"), ik[:], "ik")
                for y in range(2):
                    for part, c in PARTS:
                        act.wait_ge(*on("proj", (L, "iq", y), part))
                        for h in range(2):
                            copy(iq[:, 2 * y + h, c], psum[h * ID:(h + 1) * ID, bank_of("proj", (L, "iq", y), part), 0:HC])\
                                .then_inc(*sig("iq", (L, "iq", y), part))
                act.wait_ge(*on("ikwT", L, 0))
                copy(ikw[:, 0:NP_T, :], psum[:, bank_of("ikwT", L, 0), :].rearrange("p (t n) -> p t n", t=NP_T)
                     [:, :, 0:ID + IH]).then_inc(*sig("ikw", L, 0))
                act.wait_ge(*on("ikwT", L, 1))
                copy(ikw[0:NS, SMP, :], psum[0:NS, bank_of("ikwT", L, 1), 0:ID + IH]).then_inc(*sig("ikw", L, 1))
                act.wait_ge(*on("ikw", L, 1))
                act.dma_start(idxk_rows_prompt[0, 0].rearrange("(t p) d -> p t d", p=P), ikw[:, 0:NP_T, 0:ID])\
                    .then_inc(*sig("stores_ik", 0, n=16))
                act.dma_start(idxk_rows_sample[0].rearrange("b q d -> (b q) d"), ikw[0:NS, SMP, 0:ID])\
                    .then_inc(*sig("stores_ik", 1, n=16))
                sc = ID ** -0.5 * IH ** -0.5
                n = 0
                for t in range(1, NP_T):
                    for h in range(IH):
                        act.wait_ge(*on("idx", L, t, h))
                        if n >= 2:
                            act.wait_ge(*on("relu_used", L, n - 2))
                        act.activation(relu_p[:, n % 2, 0:(t + 1) * P], psum[:, bank_of("idx", L, t, h), 0:(t + 1) * P],
                                       ACT.Relu, scale=sc).then_inc(*sig("idx_relu", L, t, h))
                        n += 1
                def k_rows(n):
                    for t in range(TILES):
                        if n:
                            act.wait_ge(*on("dkT", L, 0, t))
                            act.wait_ge(*on(f"stores_k{t}", 0))
                        t_out((L, "k", n), t, k_st[0:rows(t), t, :], "k_st")
                        act.wait_ge(*on("k_st", (L, "k", n), t))
                        dst = k_rows_prompt[0, 0, t * P:(t + 1) * P] if t < NP_T \
                            else k_rows_sample[0].rearrange("b q h e -> (b q) h e")
                        act.dma_start(dst.rearrange("t h e -> t (h e)")[:, n * BLK:(n + 1) * BLK],
                                      k_st[0:rows(t), t, :]).then_inc(*sig(f"stores_k{t}", n, n=16))

                k_rows(0)
                for c in range(2):
                    for b in range(DB):
                        act.wait_ge(*on("idx_turned", L, c, b))
                        if (c, b) >= (0, 2):
                            q = c * DB + b - 2
                            act.wait_ge(*on("idx_s", L, q // DB, q % DB))
                        copy(ik_old[:, b % 2, :], psum[0:ID, bank_of("oldT", L, c, b), :])\
                            .then_inc(*sig("ik_old", L, c, b))
                    act.wait_ge(*on("idx_s", L, c))
                    act.activation(relu_s[:, c * BLK:(c + 1) * BLK], psum[:, c, :], ACT.Relu, scale=sc)\
                        .then_inc(*sig("idx_relu_s", L, c))
                act.wait_ge(*on("idx_s", L, 2))
                act.activation(relu_s[:, PAST:KEYS], psum[:, 2, 0:NS], ACT.Relu, scale=sc)\
                    .then_inc(*sig("idx_relu_s", L, 2))

                def k_turned(n):
                    for t in range(TILES):
                        act.wait_ge(*on("dkT", L, n, t))
                        src = psum[:, bank_of("dkT", L, n, t), :].rearrange("p (h t) -> p h t", h=4)[:, :, 0:rows(t)]
                        dst = k_d[:, 4 * n:4 * n + 4, cols(t)] if t < NP_T else ks_d[:, 4 * n:4 * n + 4, :]
                        copy(dst, src).then_inc(*sig("k_d", L, n, t))

                def q_out(x):
                    for h in (2 * x, 2 * x + 1):
                        f_out((L, "q", h), q_d[:, h, :], "q_d", sample=qs_d[:, h, :])

                q_out(0)
                k_turned(0)
                k_rows(1)
                q_out(1)
                k_turned(1)
                q_out(2)
                q_out(3)
                act.wait_ge(*on("score_s", L, 2))
                for n in range(2):
                    for t in range(TILES):
                        t_out((L, "v", n), t, v_d[0:rows(t), t, n * BLK:(n + 1) * BLK], "v_d")
                        if n:
                            act.wait_ge(*on("v_d", (L, "v", n), t))
                            dst = v_rows_prompt[0, 0, t * P:(t + 1) * P] if t < NP_T \
                                else v_rows_sample[0].rearrange("b q h e -> (b q) h e")
                            act.dma_start(dst.rearrange("t h e -> t (h e)"), v_d[0:rows(t), t, :])\
                                .then_inc(*sig("stores_v", t, n=16))
                for k in range(KT):
                    gate(L, gate_d, k)
                act.preload_act_table_set(EXP_LN)

                units = [(t, h) for t in range(NP_T) for h in range(DH)]
                for t in range(TILES):
                    act.wait_ge(*on(f"stores_k{t}", 1))

                def pt_out(n):
                    t, h = units[n]
                    act.wait_ge(*on("PT", L, n))
                    if n >= 2:
                        act.wait_ge(*on("O", L, n - 2))
                    copy(pt_at[:, n % 2, 0:(t + 1) * P], psum[:, bank_of("PT", L, n), 0:(t + 1) * P])\
                        .then_inc(*sig("PT_read", L, n))

                def branch_hi(m):
                    t, h = units[4 * m]
                    act.wait_ge(*on("oT_read", L, t, h // 4))
                    copy(h_hi[:, h:h + 4, cols(t)], tmp_d[:].rearrange("p (k t) -> p k t", k=4))\
                        .then_inc(*sig("h_hi", (L, "out"), t, h // 4))

                for n in range(len(units) + 4):
                    if n < len(units):
                        t, h = units[n]
                        act.wait_ge(*on("s_shift", L, n))
                        if n >= 3:
                            act.wait_ge(*on("PT", L, n - 3))
                        act.activation(p_at[:, n % 3, 0:(t + 1) * P], s_at[:, n % 2, 0:(t + 1) * P], ACT.Exp,
                                       bias=ast[:, n % 2, 1:2], scale=HD ** -0.5,
                                       accum_out=ast[:, n % 2, 2:3]).then_inc(*sig("p_exp", L, n))
                    if 2 <= n <= len(units) + 1:
                        pt_out(n - 2)
                    if n >= 7 and n % 4 == 3:
                        branch_hi((n - 7) // 4)

                def keys_out(i):
                    act.wait_ge(*on("pages_used", L, "kT", i))
                    if i >= 4:
                        act.wait_ge(*on("key_scores", L, i - 4))
                    copy(kt_s[:, (i // 2) % 2, 0:4, :],
                         psum[:, bank_of("KT", L, i), :].rearrange("p (h t) -> p h t", h=4)).then_inc(*sig("kt_s0", L, i))

                def sample_exp(grp):
                    act.wait_ge(*on("ss_shift", L, grp))
                    if grp:
                        act.wait_ge(*on("OsT", L, 0, 1))
                    act.activation(p_s[:], wide[:, 0:KEYS], ACT.Exp, bias=ast[:, 0, 1:2], scale=HD ** -0.5,
                                   accum_out=ast[:, 0, 2:3]).then_inc(*sig("ss_read", L, grp))

                def probs_out(grp):
                    for x in range(3):
                        act.wait_ge(*on("PsT", L, grp, x))
                        if grp:
                            act.wait_ge(*on("Os", L, 0))
                        b = bank_of("PsT", L, grp, x)
                        if x < 2:
                            copy(pt_s[:, 4 * x:4 * x + 4, :], psum[:, b, :].rearrange("p (g r) -> p g r", g=4))\
                                .then_inc(*sig("pt_s", L, grp, x))
                        else:
                            copy(ptn_s[:], psum[0:NS, b, 0:P]).then_inc(*sig("pt_s", L, grp, x))

                def rows_out(grp):
                    act.wait_ge(*on("Os", L, grp))
                    copy(p_s[:, 0:BLK], psum[:, 3, :]).then_inc(*sig("o_full0", L, grp))

                n_half = 2 * DB * NPAGE
                for i in range(0, n_half, 2):
                    keys_out(i)
                    if i == n_half // 2 - 2:
                        sample_exp(0)
                    if i == n_half // 2 + 2:
                        probs_out(0)
                rows_out(0)
                sample_exp(1)
                probs_out(1)
                rows_out(1)
                act.wait_ge(*on("os_read", L, 1, 1))
                copy(h_hi[:, :, SEQ:TOK], tmp_d2[:].rearrange("p (h t) -> p h t", h=DH))\
                    .then_inc(*sig("h_hi", (L, "out"), SMP, 1))

            def pooling(L):
                norm(L)
                act.wait_ge(*on("stores_v", "all"))
                act.wait_ge(*on("stores_ik", "all"))
                for half in range(2):
                    act.wait_ge(*on("oldP", L, half))
                    src = psum[:, bank_of("oldP", L, half), :].rearrange("p (k r) -> p k r", k=4)
                    for k in range(4):
                        copy(u_s[:, 4 * half + k, :, 1:PADW],
                             src[:, k, 0:DB * STATE].rearrange("p (b r) -> p b r", b=DB))\
                            .then_inc(*sig("u_old", L, half))
                for n in range(2 * KT):
                    if n < KT:
                        f_out((L, "u", n), u_p[:, n, PADW:], "u", sample=u_new[:, n, :])
                        act.wait_ge(*on("u", (L, "u", n), 1))
                        copy(u_s[:, n, :, PADW:], u_new[:, n, :].rearrange("p (b q) -> p b q", b=DB))\
                            .then_inc(*sig("u_placed", L, n))
                    else:
                        gate(L, gate_p, n - KT)
                    if 2 <= n < KT + 2:
                        act.wait_ge(*on("d_tmp", L, n - 2))
                        copy(d_hi[:, n - 2, :], d_tmp[n % 2][:]).then_inc(*sig("d_hi", L, n - 2))
                act.preload_act_table_set(EXP_LN)
                for part, m in ((0, STATE), (1, NS)):
                    for half in range(2):
                        act.wait_ge(*on("rowsT", L, part, half))
                        copy(new_rows[0:m, part, half * BLK:(half + 1) * BLK],
                             psum[0:m, bank_of("rowsT", L, part, half), :]).then_inc(*sig("pool_rows", L, part, half))
                act.wait_ge(*on("pool_rows", L, 1, 1))
                act.dma_start(pool_state_prompt[0, 0], new_rows[0:STATE, 0, :]).then_inc(*sig("stores_pool", 0, n=16))
                for b in range(DB):
                    act.dma_start(pool_state_sample[0, b, STATE - DQ:, :], new_rows[b * DQ:(b + 1) * DQ, 1, :])\
                        .then_inc(*sig("stores_pool", 1, b, n=16))
                act.dma_start(pool_state_sample[0, :, 0:STATE - DQ, :], state_pool[0, :, DQ:, :])\
                    .then_inc(*sig("stores_pool", 2, n=16))
                for k in range(KT):
                    act.wait_ge(*on("y_read", (L, "y", k), 1))
                    copy(h_hi[:, k, :], d_tmp[k % 2][:]).then_inc(*sig("y_hi", L, k))

            act.preload_act_table_set(EXP_LN)
            act.wait_ge(*on("const", "first"))
            for L, kind in enumerate(KINDS):
                (gla, dsa, pooling)[kind](L)
            norm(len(KINDS), last=True)

        @block.vector
        def _(dve):
            def link(ins, name="vec_chain"):
                ins.then_inc(*sig(name, count.get(name, 0)))
                dve.wait_ge(semaphore(name), count[name])

            def refine(m, sq, y, a, b, out, n_inv, key, last_key):
                link(dve.tensor_scalar(m, sq, n_inv, RMS_EPS, ALU.mult, ALU.add))
                dve.wait_ge(*on("rstd_y", *key))
                link(dve.tensor_tensor(a, y, m, ALU.mult))
                link(dve.tensor_tensor(a, a, y, ALU.mult))
                link(dve.tensor_scalar(b, a, -0.5, 1.5, ALU.mult, ALU.add))
                link(dve.tensor_tensor(out, y, b, ALU.mult))

            def norm_lo(L, t):
                r = rows(t)
                for half in range(2):
                    dve.wait_ge(*on("h_hi", L, t, half))
                    b = bank_of("nT", L, t, half)
                    k = slice(4 * half, 4 * half + 4)
                    dve.tensor_tensor(h_lo[:, k, cols(t)],
                                      psum[:, b, :].rearrange("p (k t) -> p k t", k=4)[:, :, 0:r],
                                      h_hi[:, k, cols(t)].bitcast(F32), ALU.subtract)\
                        .then_inc(*sig("h_lo", L, t, half))

            def norm_tile(L, t):
                last = L == len(KINDS)
                r = rows(t)
                s = st[0:r, t % 2, :]
                if t == 0:
                    dve.wait_ge(*on("gain", L))
                rest_first = t and not last and (L == 0 or t == NP_T - 1)
                if rest_first:
                    norm_lo(L, t - 1)
                dve.wait_ge(*on("sumsq", L, t))
                refine(s[:, 1:2], s[:, 0:1], s[:, 3:4], s[:, 4:5], s[:, 5:6], s[:, 6:7], 1.0 / D, (L, t), None)
                if t >= 2:
                    if last:
                        dve.wait_ge(*on(f"stores_y{t % 2}", t - 2))
                    else:
                        dve.wait_ge(*on("nT", L, t - 2, 1))
                dve.scalar_tensor_tensor(out=xn[0:r, t % 2, :], in0=X[0:r, t, :], scalar=s[:, 6:7],
                                         in1=gain[0:r, :], op0=ALU.mult, op1=ALU.mult).then_inc(*sig("xn", L, t))
                if not last:
                    for done in ([t - 1] if t and not rest_first else []) + ([SMP] if t == SMP else []):
                        norm_lo(L, done)

            def resid(L):
                for n in range(2):
                    for t in range(TILES):
                        r = rows(t)
                        name = (L, "out", n)
                        dve.wait_ge(*on("proj", (name, t)))
                        x = X[0:r, t, n * BLK:(n + 1) * BLK]
                        dve.tensor_tensor(x, psum[0:r, bank_of("proj", name, t), :], x, ALU.add)\
                            .then_inc(*sig("resid", name, t))
                        if n and t:
                            norm_tile(L + 1, t - 1)
                norm_tile(L + 1, SMP)

            def out_gated(L, t, half, gate_buf, tmp):
                n = rows(t)
                dve.tensor_tensor(tmp.rearrange("p (k t) -> p k t", k=4),
                                  psum[:, bank_of("oT", L, t, half), :].rearrange("p (k t) -> p k t", k=4)[:, :, 0:n],
                                  gate_buf[:, 4 * half:4 * half + 4, cols(t)], ALU.mult)\
                    .then_inc(*sig("oT_read", L, t, half))

            def out_lo(L, t, half, tmp):
                k = slice(4 * half, 4 * half + 4)
                dve.wait_ge(*on("h_hi", (L, "out"), t, half))
                dve.tensor_tensor(h_lo[:, k, cols(t)], tmp.rearrange("p (k t) -> p k t", k=4),
                                  h_hi[:, k, cols(t)].bitcast(F32), ALU.subtract)\
                    .then_inc(*sig("h_lo", (L, "out"), t, half))

            def gla(L):
                dve.wait_ge(*on("const", "all"))
                dve.wait_ge(*on("gla_small", L))
                if L:
                    dve.wait_ge(*on("stores_pool", "all"))
                for h in range(GH):
                    dve.wait_ge(*on("z_abs", L, h))
                    dve.tensor_scalar(qg[:, h, 0:SEQ], psum[:, bank_of("z", L, h), :], b_a[:, h:h + 1], 0.0,
                                      ALU.add, ALU.min).then_inc(*sig("z_read", L, h))
                dve.wait_ge(*on("z_abs", L, "s"))
                for h in range(GH):
                    dve.tensor_scalar(qg[:, h, SEQ:TOK], psum[:, bank_of("z", L, "s"), h * NS:(h + 1) * NS],
                                      b_a[:, h:h + 1], 0.0, ALU.add, ALU.min).then_inc(*sig("z_read", L, "s"))
                dve.wait_ge(*on("z_read", L, "s"))
                dve.wait_ge(*on("z_soft", L))
                link(dve.tensor_tensor(qg[:], qg[:], soft[:], ALU.subtract))
                for h in range(GH):
                    ins = dve.tensor_tensor_scan(kg[:, h, :], no_reset[:], qg[:, h, :], 0.0, ALU.mult, ALU.add)
                    if h < GH - 1:
                        ins.then_inc(*sig("vec_chain", count.get("vec_chain", 0)))
                link(ins)
                kc = kg[:, :, 0:SEQ].rearrange("p h (c t) -> p h c t", c=NCH)
                qc = qg[:, :, 0:SEQ].rearrange("p h (c t) -> p h c t", c=NCH)
                link(dve.tensor_copy(mid[:], kc[:, :, :, CH // 2 - 1]))
                for h in range(GH):
                    dve.tensor_tensor(qc[:, h], kc[:, h], mid[:, h, :].unsqueeze(2).broadcast_to([P, NCH, CH]),
                                      ALU.subtract).then_inc(*sig("decay_h", L, h))
                dve.tensor_copy(qg[:, :, SEQ:TOK], kg[:, :, SEQ:TOK]).then_inc(*sig("decay_h", L, "s"))
                dve.wait_ge(*on("decay_h", L, "s"))
                dve.tensor_tensor(fac[:, :, 0:NCH - 1], qc[:, :, 0:NCH - 1, CH - 1], mid[:, :, 1:NCH], ALU.add)\
                    .then_inc(*sig("fac_part", L, 0))
                dve.tensor_copy(fac[:, :, NCH - 1:NCH], qc[:, :, NCH - 1:NCH, CH - 1])\
                    .then_inc(*sig("fac_part", L, 1))
                dve.tensor_copy(fac[:, :, NCH:], kg[:, :, SEQ:TOK].rearrange("p h (b q) -> p h b q", b=DB)[:, :, :, DQ - 1])\
                    .then_inc(*sig("fac", L, also=()))
                dve.wait_ge(*on("fac", L))
                dve.tensor_copy(mid[:, :, 0:1], mid[:, :, 0:1]).then_inc(*sig("decay", L))
                dve.wait_ge(*on("k_decay", L))
                for h in range(GH):
                    name = (L, "k", h)
                    for part, c in PARTS:
                        dve.wait_ge(*on("proj", name, part))
                        dve.tensor_tensor(kg[:, h, c], psum[:, bank_of("proj", name, part), 0:HC],
                                          kg[:, h, c], ALU.mult).then_inc(*sig("k_gated", name, part))
                dve.wait_ge(*on("q_decay", L))
                for h in range(GH):
                    name = (L, "q", h)
                    for part, c in PARTS:
                        dve.wait_ge(*on("proj", name, part))
                        dve.scalar_tensor_tensor(out=qg[:, h, c],
                                                 in0=psum[:, bank_of("proj", name, part), 0:HC],
                                                 scalar=GDK ** -0.5, in1=qg[:, h, c], op0=ALU.mult,
                                                 op1=ALU.mult).then_inc(*sig("q_gated", name, part))
                dve.wait_ge(*on("q_gated", (L, "q", GH - 1), 1))
                for h in range(GH):
                    dve.tensor_tensor(q_seq[:, h], qg[:, h, SEQ:TOK].unsqueeze(1).broadcast_to([P, DB, NS]),
                                      seq_col[:], ALU.mult).then_inc(*sig("q_seq", L))

                def add_state(c):
                    dve.wait_ge(*on("state", L, c))
                    b = bank_of("state", L, c, 0)
                    src = wide[:, b * 512:b * 512 + GH * GDV]
                    if c == 0:
                        dve.tensor_copy(s_sum[:], src).then_inc(*sig("s_sum", L, c))
                    else:
                        dve.wait_ge(*on("s_now", L, c))
                        dve.tensor_tensor(s_sum[:], src, s_now[:, c % 2, :], ALU.add).then_inc(*sig("s_sum", L, c))

                def out_rows(t):
                    r = rows(t)
                    dve.wait_ge(*on("o", L, t))
                    b = bank_of("o", L, t, 0)
                    dve.tensor_copy(v_g[0:r, t, :], wide[0:r, b * 512:b * 512 + D]).then_inc(*sig("o_out", L, t))

                def normalise(t):
                    r = rows(t)
                    for h in range(GH):
                        x = v_g[0:r, t, h * GDV:(h + 1) * GDV]
                        dve.scalar_tensor_tensor(out=x, in0=x, scalar=ost[0:r, 4, 4 * t + h:4 * t + h + 1],
                                                 in1=g_on[0:r, :], op0=ALU.mult, op1=ALU.mult)\
                            .then_inc(*sig("o_norm", L, t))

                dve.wait_ge(*on("att", L, SMP))
                dve.tensor_tensor(att_g[0:NS, :, 0:NS], psum[0:NS, 0, 0:GH * NS].rearrange("p (h t) -> p h t", h=GH),
                                  seq_tri[:].unsqueeze(1).broadcast_to([NS, GH, NS]), ALU.mult)\
                    .then_inc(*sig("att_m", L, SMP))

                def k_of(b):
                    if b >= 2:
                        dve.wait_ge(*on("s_state", L, b - 2))
                    dve.tensor_scalar(k_seq[:, b % 2, :], k_tok[0:NS, SMP, :], seq_row[:, b:b + 1], None, ALU.mult)\
                        .then_inc(*sig("k_seq", L, b))

                def sequence(b):
                    dve.wait_ge(*on("s_state", L, b))
                    pb = bank_of("s_state", L, b, 0)
                    dve.tensor_tensor(s_in[:, b % 3].rearrange("p h v -> p (h v)"), wide[:, pb * 512:pb * 512 + D],
                                      s_in[:, b % 3].rearrange("p h v -> p (h v)"), ALU.add)\
                        .then_inc(*sig("s_new", L, b))
                    if b + 2 < DB:
                        k_of(b + 2)

                dve.wait_ge(*on("k_tok", L, SMP))
                k_of(0)
                k_of(1)
                for t in range(NP_T):
                    dve.wait_ge(*on("att", L, t))
                    dve.tensor_tensor(att_g[:], psum[:, 0, :].rearrange("p (h t) -> p h t", h=GH),
                                      chunk_tri[:].unsqueeze(1).broadcast_to([P, GH, P]), ALU.mult)\
                        .then_inc(*sig("att_m", L, t))
                    add_state(2 * t)
                    sequence(2 * t)
                    add_state(2 * t + 1)
                    sequence(2 * t + 1)
                    out_rows(t)
                dve.wait_ge(*on("o", L, SMP))
                for part in range(2):
                    dve.tensor_copy(v_g[0:NS, SMP, part * BLK:(part + 1) * BLK], psum[part * NS:(part + 1) * NS, 7, :])\
                        .then_inc(*sig("o_out", L, SMP))
                for c, tiles, key in ((slice(0, 12), range(NP_T - 1), 0), (slice(12, 16), (NP_T - 1,), 2)):
                    dve.wait_ge(*on("o_sq", L, tiles[-1]))
                    refine(ost[:, 1, c], ost[:, 0, c], ost[:, 3, c], ost[:, 1, c], ost[:, 2, c], ost[:, 4, c],
                           1.0 / GDV, (L, "o", key), None)
                    for t in tiles:
                        normalise(t)
                dve.wait_ge(*on("o_sq", L, SMP))
                c = slice(16, 20)
                refine(ost[0:NS, 1, c], ost[0:NS, 0, c], ost[0:NS, 3, c], ost[0:NS, 1, c], ost[0:NS, 2, c],
                       ost[0:NS, 4, c], 1.0 / GDV, (L, "o", 1), None)
                normalise(SMP)
                for t in range(TILES):
                    for half in range(2):
                        dve.wait_ge(*on("oT", L, t, half))
                        if t:
                            dve.wait_ge(*on("h_lo", (L, "out"), t - 1, half))
                        out_gated(L, t, half, gate_g, tmp_og[:, half, 0:4 * rows(t)])
                    for half in range(2):
                        out_lo(L, t, half, tmp_og[:, half, 0:4 * rows(t)])
                resid(L)

            def dsa(L):
                for s in range(3):
                    dve.wait_ge(*on(f"s_stored{s}", L - 1, max(b for b in range(DB) if b % 3 == s)))
                dve.wait_ge(*on("stores_gla", L - 1))
                dve.wait_ge(*on("iq", (L, "iq", 1), 1))
                for h in range(IH):
                    dve.tensor_tensor(iq_seq[:, h], iq[:, h, SEQ:TOK].unsqueeze(1).broadcast_to([ID, DB, NS]),
                                      seq_col[0:ID], ALU.mult).then_inc(*sig("iq_seq", L))
                dve.wait_ge(*on("ikw", L, 1))
                for h in range(IH):
                    link(dve.tensor_copy(w_stack[h * NS:(h + 1) * NS, :], ikw[0:NS, SMP, ID + h:ID + h + 1]))
                dve.tensor_scalar(w_sel[:], stack4[:], w_stack[:], None, ALU.mult).then_inc(*sig("w_sel", L))
                n = 0
                for t in range(1, NP_T):
                    w = (t + 1) * P
                    for h in range(IH):
                        dve.wait_ge(*on("idx_relu", L, t, h))
                        s = ikw[:, t, ID + h:ID + h + 1]
                        if h == 0:
                            ins = dve.tensor_scalar(bias_p[t][:], relu_p[:, n % 2, 0:w], s, None, ALU.mult)
                        else:
                            ins = dve.scalar_tensor_tensor(out=bias_p[t][:], in0=relu_p[:, n % 2, 0:w], scalar=s,
                                                           in1=bias_p[t][:], op0=ALU.mult, op1=ALU.add)
                        ins.then_inc(*sig("relu_used", L, n))
                        dve.wait_ge(*on("relu_used", L, n))
                        n += 1
                    diag = bias_p[t][:, t * P:(t + 1) * P]
                    link(dve.tensor_tensor(diag, diag, future_p[:], ALU.add))
                for c, w in enumerate((BLK, BLK, NS)):
                    dve.wait_ge(*on("score_mm", L, c))
                    src = psum[0:NS, bank_of("score_s", L, c), 0:w]
                    dst = score_s[:, c * BLK:c * BLK + w]
                    if c < 2:
                        dve.tensor_copy(dst, src).then_inc(*sig("score_s", L, c))
                    else:
                        dve.tensor_tensor(dst, src, future_s[:], ALU.add).then_inc(*sig("score_s", L, c))
                dve.wait_ge(*on("score_s", L, 2))

                def top(scores, m, k):
                    for _ in range(k // 8):
                        link(dve.max(out=top8[0:m, :], in_=scores))
                        link(dve.match_replace(out=scores, in_to_replace=top8[0:m, :], in_values=scores,
                                               imm_value=TAKEN))

                for t in range(1, NP_T):
                    top(bias_p[t][:], P, TOPK_P)
                    link(dve.tensor_scalar(bias_p[t][:], bias_p[t][:], TAKEN, FUTURE, ALU.not_equal, ALU.mult))
                top(score_s[:], NS, TOPK_S)
                dve.tensor_scalar(bias_s[:], score_s[:], TAKEN, FUTURE, ALU.not_equal, ALU.mult)\
                    .then_inc(*sig("bias_s", L))

                units = [(t, h) for t in range(NP_T) for h in range(DH)]
                for t in range(TILES):
                    dve.wait_ge(*on(f"stores_k{t}", 1))
                dve.wait_ge(*on("dkT", L, 1, SMP))

                def shift(n):
                    t, h = units[n]
                    w = (t + 1) * P
                    dve.wait_ge(*on("S", L, n))
                    if n >= 2:
                        dve.wait_ge(*on("p_exp", L, n - 2))
                    dve.tensor_tensor_reduce(out=s_at[:, n % 2, 0:w], in0=psum[:, bank_of("S", L, n), 0:w],
                                             in1=(bias_p[t][:] if t else future_p[:]), scale=1.0, scalar=TAKEN,
                                             op0=ALU.add, op1=ALU.max, accum_out=ast[:, n % 2, 0:1])\
                        .then_inc(*sig("S_read", L, n))
                    dve.wait_ge(*on("S_read", L, n))
                    dve.tensor_scalar(ast[:, n % 2, 1:2], ast[:, n % 2, 0:1], -HD ** -0.5, None, ALU.mult)\
                        .then_inc(*sig("s_shift", L, n))

                def normalise(n):
                    t, h = units[n]
                    dve.wait_ge(*on("p_exp", L, n))
                    link(dve.reciprocal(ast[:, n % 2, 3:4], ast[:, n % 2, 2:3]))
                    x = p_at[:, n % 3, 0:(t + 1) * P]
                    dve.tensor_scalar(x, x, ast[:, n % 2, 3:4], None, ALU.mult).then_inc(*sig("p_norm", L, n))

                def branch(m):
                    t, h = units[4 * m]
                    dve.wait_ge(*on("O", L, 4 * m + 3))
                    if m:
                        pt, ph = units[4 * m - 4]
                        dve.wait_ge(*on("h_lo", (L, "out"), pt, ph // 4))
                    dve.tensor_tensor(tmp_d[:].rearrange("p (k t) -> p k t", k=4),
                                      psum[:, (4, 5)[m % 2], :].rearrange("p (k t) -> p k t", k=4),
                                      gate_d[:, h:h + 4, cols(t)], ALU.mult).then_inc(*sig("oT_read", L, t, h // 4))
                    out_lo(L, t, h // 4, tmp_d[:])

                for n in range(len(units) + 4):
                    if n < len(units):
                        shift(n)
                    if 1 <= n <= len(units):
                        normalise(n - 1)
                    if n >= 7 and n % 4 == 3:
                        branch((n - 7) // 4)

                dve.wait_ge(*on("S", L, len(units) - 1))
                link(dve.memset(q_heads[:], 0.0))
                for h in range(DH):
                    dve.tensor_copy(q_heads[:, h, :, h * DQ:(h + 1) * DQ],
                                    qs_d[:, h, :].rearrange("p (b q) -> p b q", b=DB)).then_inc(*sig("q_heads", L))
                def keys_out(i):
                    dve.wait_ge(*on("pages_used", L, "kT", i))
                    if i >= 4:
                        dve.wait_ge(*on("key_scores", L, i - 4))
                    dve.tensor_copy(kt_s[:, (i // 2) % 2, 4:8, :],
                                    psum[:, bank_of("KT", L, i), :].rearrange("p (h t) -> p h t", h=4))\
                        .then_inc(*sig("kt_s1", L, i))

                def sample_max(grp):
                    dve.wait_ge(*on("SS", L, grp))
                    link(dve.tensor_reduce(ast[:, 0, 0:1], wide[:, 0:KEYS], AX.X, ALU.max))
                    dve.tensor_scalar(ast[:, 0, 1:2], ast[:, 0, 0:1], -HD ** -0.5, None, ALU.mult)\
                        .then_inc(*sig("ss_shift", L, grp))

                def sample_norm(grp):
                    dve.wait_ge(*on("ss_read", L, grp))
                    link(dve.reciprocal(ast[:, 0, 3:4], ast[:, 0, 2:3]))
                    dve.tensor_scalar(p_s[:], p_s[:], ast[:, 0, 3:4], None, ALU.mult).then_inc(*sig("ps_norm", L, grp))

                def rows_out(grp):
                    dve.wait_ge(*on("Os", L, grp))
                    dve.tensor_copy(p_s[:, BLK:D], psum[:, 4, :]).then_inc(*sig("o_full1", L, grp))

                def sample_branch(grp):
                    c = slice(grp * 4 * DQ, (grp + 1) * 4 * DQ)
                    for h in range(DH):
                        dve.wait_ge(*on("OsT", L, grp, h // 4))
                        dve.tensor_tensor(
                            tmp_d2[:, h * NS:(h + 1) * NS][:, c].rearrange("p (b q) -> p b q", b=4),
                            psum[:, bank_of("OsT", L, grp, h // 4), (h % 4) * P:(h % 4 + 1) * P]
                            .rearrange("p (b g q) -> p b g q", b=4, g=DH)[:, :, h, :],
                            gate_d[:, h, SEQ:TOK][:, c].rearrange("p (b q) -> p b q", b=4), ALU.mult)\
                            .then_inc(*sig("os_read", L, grp, h // 4))

                n_half = 2 * DB * NPAGE
                for i in range(1, n_half, 2):
                    keys_out(i)
                    if i == n_half // 2 - 1:
                        sample_max(0)
                    if i == n_half // 2 + 1:
                        sample_norm(0)
                rows_out(0)
                sample_max(1)
                sample_branch(0)
                sample_norm(1)
                rows_out(1)
                sample_branch(1)
                dve.wait_ge(*on("os_read", L, 1, 1))
                dve.wait_ge(*on("h_hi", (L, "out"), SMP, 1))
                dve.tensor_tensor(h_lo[:, :, SEQ:TOK], tmp_d2[:].rearrange("p (h t) -> p h t", h=DH),
                                  h_hi[:, :, SEQ:TOK].bitcast(F32), ALU.subtract)\
                    .then_inc(*sig("h_lo", (L, "out"), SMP, 1))
                resid(L)

            def pooling(L):
                dve.wait_ge(*on("stores_v", "all"))
                dve.memset(u_p[:, :, 0:PADW], 0.0).then_inc(*sig("u_pad", L))
                dve.wait_ge(*on("u_pad", L))
                link(dve.reciprocal(inv_cnt[:], inv_cnt[:]))
                dve.wait_ge(*on("pool_small"))
                dve.wait_ge(*on("u_old", L, 1))
                for k in range(KT):
                    grp = k // 2
                    w = WINDOWS[grp]
                    tmp = d_tmp[k % 2]
                    dve.wait_ge(*on("u_placed", L, k))
                    src, src_s = u_p[:, k, :], u_s[:, k]
                    for i in range(grp + 1):
                        s = 1 << i
                        dst, dst_s = win[:, i % 2, :], win_s[:, i % 2]
                        dve.tensor_tensor(dst[:, 2 * s - 1:], src[:, 2 * s - 1:], src[:, s - 1:PADW + SEQ - s],
                                          ALU.add).then_inc(*sig("vec_chain", count.get("vec_chain", 0)))
                        link(dve.tensor_tensor(dst_s[:, :, 2 * s:], src_s[:, :, 2 * s:],
                                               src_s[:, :, s:PADW + DQ - s], ALU.add))
                        src, src_s = dst, dst_s
                    if k >= 2:
                        dve.wait_ge(*on("d_lo", L, k - 2))
                    dve.scalar_tensor_tensor(out=tmp[:, 0:SEQ], in0=src[:, PADW:], scalar=1.0 / w,
                                             in1=u_p[:, k, PADW:], op0=ALU.mult, op1=ALU.subtract)\
                        .then_inc(*sig("vec_chain", count.get("vec_chain", 0)))
                    dve.tensor_tensor(small_d[:, 0:w - 1], src[:, PADW:PADW + w - 1], inv_cnt[:, 0:w - 1], ALU.mult)\
                        .then_inc(*sig("vec_chain", count.get("vec_chain", 0)))
                    link(dve.scalar_tensor_tensor(out=tmp[:, SEQ:TOK].rearrange("p (b q) -> p b q", b=DB),
                                                  in0=src_s[:, :, PADW:], scalar=1.0 / w, in1=u_s[:, k, :, PADW:],
                                                  op0=ALU.mult, op1=ALU.subtract))
                    dve.tensor_tensor(tmp[:, 0:w - 1], small_d[:, 0:w - 1], u_p[:, k, PADW:PADW + w - 1],
                                      ALU.subtract).then_inc(*sig("d_tmp", L, k))
                    for done in ([k - 1] if k else []) + ([k] if k == KT - 1 else []):
                        dve.wait_ge(*on("d_hi", L, done))
                        dve.tensor_tensor(d_lo[:, done, :], d_tmp[done % 2][:], d_hi[:, done, :].bitcast(F32),
                                          ALU.subtract).then_inc(*sig("d_lo", L, done))
                dve.wait_ge(*on("gate", (L, "g", KT - 1), 1))
                dve.wait_ge(*on("d_lo", L, KT - 1))
                for k in range(KT):
                    name = (L, "y", k)
                    if k >= 2:
                        dve.wait_ge(*on("h_lo", L, "y", k - 2))
                    for part, c in PARTS:
                        dve.wait_ge(*on("proj", name, part))
                        dve.scalar_tensor_tensor(out=d_tmp[k % 2][:, c],
                                                 in0=psum[:, bank_of("proj", name, part), 0:HC],
                                                 scalar=scale_p[:, k:k + 1], in1=gate_p[:, k, c], op0=ALU.mult,
                                                 op1=ALU.mult).then_inc(*sig("y_read", name, part))
                    for done in ([k - 1] if k else []) + ([k] if k == KT - 1 else []):
                        dve.wait_ge(*on("y_hi", L, done))
                        dve.tensor_tensor(h_lo[:, done, :], d_tmp[done % 2][:], h_hi[:, done, :].bitcast(F32),
                                          ALU.subtract)\
                            .then_inc(*sig("h_lo", L, "y", done,
                                           also=[((L, "out"), t, 1) for t in range(TILES)] if done == KT - 1 else ()))
                resid(L)

            dve.wait_ge(*on("const", "first"))
            for t in range(TILES):
                norm_tile(0, t)
            for L, kind in enumerate(KINDS):
                (gla, dsa, pooling)[kind](L)


_INS = ["x_prompt", "x_sample", "state_gla", "cache_k", "cache_v", "cache_idx_k", "state_pool", "page_table",
        "gla_norm", "gla_w_in", "gla_w_a2", "gla_b_a", "gla_out_norm", "gla_w_out", "dsa_norm", "dsa_w_in",
        "dsa_w_out", "pool_norm", "pool_w_in", "pool_w_grp", "pool_scale", "pool_w_out", "final_norm"]
_OUTS = [(1, SEQ, D), (DB, DQ, D), (2, 1, GH, GDK, GDV), (2, DB, GH, GDK, GDV), (1, 1, SEQ, DH, HD),
         (1, DB, DQ, DH, HD), (1, 1, SEQ, DH, HD), (1, DB, DQ, DH, HD), (1, 1, SEQ, ID), (1, DB, DQ, ID),
         (1, 1, STATE, D), (1, DB, STATE, D)]


def kernel(**inputs):
    import numpy as _np
    import concourse.bacc as _bacc
    from concourse import mybir as _mybir
    from concourse.bass_utils import run_bass_kernel_spmd as _run

    arrays = {f"in_{name}_dram": _np.ascontiguousarray(inputs[name]) for name in _INS}
    plan = Plan()
    for _ in range(2):
        nc = _bacc.Bacc("TRN2", target_bir_lowering=False, num_devices=1, dynamic_dma_scratch_size=1024)
        args = [nc.dram_tensor(n, a.shape, _mybir.dt.from_np(a.dtype), kind="ExternalInput").ap()
                for n, a in arrays.items()]
        outs = [nc.dram_tensor(f"out_{i}_dram", shape, _mybir.dt.float32, kind="ExternalOutput").ap()
                for i, shape in enumerate(_OUTS)]
        program(nc, plan, *args, outs)
    r = _run(nc, [arrays], core_ids=[0])
    return tuple(r.results[0][f"out_{i}_dram"] for i in range(len(_OUTS)))
```
